# Optimizing a Trainium2 kernel written in Bass

```python
import jax, jax.numpy as jnp
from jax import lax
import numpy as np

D_MODEL = 1024
BATCH = 1
SEQ = 1024
DEPTH = 2

CHUNK = 64
N_MIXERS = 2
EPS = 1e-6

SGU_BLOCK = 128
GMLP_HIDDEN = 2 * D_MODEL
SGU_GROUPS = 8
SGU_GROUP_DIM = GMLP_HIDDEN // SGU_GROUPS

N_HEADS = 16
HEAD_DIM = D_MODEL // N_HEADS
LEFT_CHUNKS = 8
BAND = (LEFT_CHUNKS + 1) * CHUNK
REL_MIN = -(CHUNK - 1)
REL_MAX = 128
N_REL = REL_MAX - REL_MIN + 1

D_FF = -(-(8 * D_MODEL) // (3 * 256)) * 256

N_A = (DEPTH + 1) // 2
N_B = DEPTH // 2

kernel_name = "hybrid_gmlp_chunkattn_trunk"

def rms_norm(x, g):
    xf = x.astype(jnp.float32)
    y = xf * lax.rsqrt(jnp.mean(xf * xf, axis=-1, keepdims=True) + EPS)
    return (y * g.astype(jnp.float32)).astype(x.dtype)

def gmlp_mixer(h, w_in, v_gain, w_s, b_s, w_out):
    bsz, seq, _ = h.shape
    uv = jax.nn.gelu(h @ w_in)
    u, v = jnp.split(uv, 2, axis=-1)
    v = rms_norm(v, v_gain)
    nb = seq // SGU_BLOCK
    v = v.reshape(bsz, nb, SGU_BLOCK, SGU_GROUPS, SGU_GROUP_DIM)
    pos = jnp.arange(SGU_BLOCK)
    mask = (pos[None, :] // CHUNK) <= (pos[:, None] // CHUNK)
    w = w_s * mask.astype(w_s.dtype)[None]
    v = jnp.einsum('gpq,bnqgc->bnpgc', w, v) + b_s.T[None, None, :, :, None]
    y = u * v.reshape(bsz, seq, GMLP_HIDDEN)
    return y @ w_out

def chunk_attention(h, w_qkv, rel_bias, w_out):
    bsz, seq, _ = h.shape
    nc = seq // CHUNK
    qkv = (h @ w_qkv).reshape(bsz, seq, 3, N_HEADS, HEAD_DIM)
    q, k, v = qkv[:, :, 0], qkv[:, :, 1], qkv[:, :, 2]
    pad = LEFT_CHUNKS * CHUNK
    kp = jnp.pad(k, ((0, 0), (pad, 0), (0, 0), (0, 0)))
    vp = jnp.pad(v, ((0, 0), (pad, 0), (0, 0), (0, 0)))
    qi = jnp.arange(CHUNK)[:, None]
    kj = jnp.arange(BAND)[None, :]
    rel_idx = jnp.clip(qi - (kj - pad), REL_MIN, REL_MAX) - REL_MIN
    bias = rel_bias[:, rel_idx].astype(jnp.float32)
    scale = HEAD_DIM ** -0.5

    def one_chunk(c):
        start = c * CHUNK
        qc = lax.dynamic_slice_in_dim(q, start, CHUNK, axis=1)
        kc = lax.dynamic_slice_in_dim(kp, start, BAND, axis=1)
        vc = lax.dynamic_slice_in_dim(vp, start, BAND, axis=1)
        s = jnp.einsum('bqhd,bkhd->bhqk', qc, kc).astype(jnp.float32) * scale + bias
        valid = kj >= pad - start
        s = jnp.where(valid[None, None], s, -jnp.inf)
        p = jax.nn.softmax(s, axis=-1).astype(vc.dtype)
        return jnp.einsum('bhqk,bkhd->bqhd', p, vc)

    o = lax.map(one_chunk, jnp.arange(nc))
    o = jnp.moveaxis(o, 0, 1).reshape(bsz, seq, N_HEADS * HEAD_DIM)
    return o @ w_out

def swiglu(h, w_gate, w_up, w_down):
    return (jax.nn.silu(h @ w_gate) * (h @ w_up)) @ w_down

def setup_inputs(seed: int = 0) -> dict:
    key = jax.random.key(seed)
    ks = jax.random.split(key, 16)
    f32 = jnp.float32

    def nrm(k, shape, scale):
        return jax.random.normal(k, shape, f32) * scale

    return {
        "x": jax.random.normal(ks[0], (BATCH, SEQ, D_MODEL), f32),
        "norm_mix_g": 1.0 + nrm(ks[1], (DEPTH, D_MODEL), 0.05),
        "norm_ffn_g": 1.0 + nrm(ks[2], (DEPTH, D_MODEL), 0.05),
        "final_g": 1.0 + nrm(ks[3], (D_MODEL,), 0.05),
        "a_w_in": nrm(ks[4], (N_A, D_MODEL, 2 * GMLP_HIDDEN), D_MODEL ** -0.5),
        "a_v_gain": 1.0 + nrm(ks[5], (N_A, GMLP_HIDDEN), 0.05),
        "a_w_s": nrm(ks[6], (N_A, SGU_GROUPS, SGU_BLOCK, SGU_BLOCK), 0.5 * SGU_BLOCK ** -0.5),
        "a_b_s": 1.0 + nrm(ks[7], (N_A, SGU_GROUPS, SGU_BLOCK), 0.1),
        "a_w_out": nrm(ks[8], (N_A, GMLP_HIDDEN, D_MODEL), GMLP_HIDDEN ** -0.5),
        "b_w_qkv": nrm(ks[9], (N_B, D_MODEL, 3 * N_HEADS * HEAD_DIM), D_MODEL ** -0.5),
        "b_rel_bias": nrm(ks[10], (N_B, N_HEADS, N_REL), 0.5),
        "b_w_out": nrm(ks[11], (N_B, N_HEADS * HEAD_DIM, D_MODEL), (N_HEADS * HEAD_DIM) ** -0.5),
        "ffn_w_gate": nrm(ks[12], (DEPTH, D_MODEL, D_FF), D_MODEL ** -0.5),
        "ffn_w_up": nrm(ks[13], (DEPTH, D_MODEL, D_FF), D_MODEL ** -0.5),
        "ffn_w_down": nrm(ks[14], (DEPTH, D_FF, D_MODEL), D_FF ** -0.5),
    }

def reference(x, norm_mix_g, norm_ffn_g, final_g, a_w_in, a_v_gain, a_w_s, a_b_s,
              a_w_out, b_w_qkv, b_rel_bias, b_w_out, ffn_w_gate, ffn_w_up, ffn_w_down):
    for i in range(DEPTH):
        j = i // N_MIXERS
        hn = rms_norm(x, norm_mix_g[i])
        if i % N_MIXERS == 0:
            x = x + gmlp_mixer(hn, a_w_in[j], a_v_gain[j], a_w_s[j], a_b_s[j], a_w_out[j])
        else:
            x = x + chunk_attention(hn, b_w_qkv[j], b_rel_bias[j], b_w_out[j])
        hn = rms_norm(x, norm_ffn_g[i])
        x = x + swiglu(hn, ffn_w_gate[i], ffn_w_up[i], ffn_w_down[i])
    return rms_norm(x, final_g)


_drawn_inputs = setup_inputs


def setup_inputs(seed=0):
    import zlib

    import numpy as np

    out = dict(_drawn_inputs(seed))
    spreads = {}
    factors = {'a_v_gain': 4.039}
    for name, (base, spread) in spreads.items():
        noise = np.random.default_rng([zlib.crc32(name.encode()), seed]).standard_normal(out[name].shape)
        drawn = base * np.exp(spread * noise) if base else spread * noise
        out[name] = __import__('jax').numpy.asarray(drawn.astype(out[name].dtype))
    for name, factor in factors.items():
        out[name] = (out[name] * factor).astype(out[name].dtype)
    return out
```

```python
from contextlib import ExitStack

import concourse.bass as bass
from concourse import mybir

F32 = mybir.dt.float32
F32R = mybir.dt.float32r
ALU = mybir.AluOpType
ACT = mybir.ActivationFunctionType

P = 128
SEQ = 1024
D = 1024
KT = D // P
HALF = SEQ // 2
NH2 = SEQ // HALF
UNIT = 1024
CHUNK = 64
EPS = 1e-6

GMLP = 2 * D
GROUPS = 8
GDIM = GMLP // GROUPS
BLOCKS = SEQ // P
CB = GMLP // 512

HEADS = 16
HD = D // HEADS
PAIRS = HEADS // 2
LEFT = 8 * CHUNK // P
WIN = (LEFT + 1) * P
N_REL = 192
REV = WIN + P - 1
MASKED = -1e30

D_FF = 2816
CHUNKS = D_FF // (2 * P)

RAW = 2
RING = 6

U_V = CB * 4
U_G = GROUPS * 4
U_F = CHUNKS * 6
U_B = PAIRS * 4
B_V, B_G = 0, U_V
B_F1 = B_G + U_G
B_B = B_F1 + U_F
B_F2 = B_B + U_B
UNITS = B_F2 + U_F


def ge(eng, sem, value):
    if isinstance(value, int) and value <= 0:
        return
    eng.wait_ge(sem, value)


def repeat(eng, n, body):
    body(0, True, False)
    with eng.Fori(1, n - 1) as it:
        body(it, False, False)
    body(n - 1, False, True)


def trunk(nc, x_t, gains, v_gain, w_s_t, b_s, rel_rev, ident_d, w_units, out_t):
    v_scratch = nc.dram_tensor("v_scratch", [BLOCKS, P, GMLP], F32).ap()
    rel_scratch_t = nc.dram_tensor("rel_scratch", [HEADS, REV], F32)
    rel_scratch = rel_scratch_t.ap()

    with ExitStack() as ctx:
        def sb(name, shape, dt=F32, at=ctx):
            return at.enter_context(nc.sbuf_tensor(name, shape, dt))

        def sem(name):
            return ctx.enter_context(nc.semaphore(name))

        bank = [ctx.enter_context(nc.psum_tensor(f"bank{i}", [P, 512], F32)) for i in range(4)]
        scores = ctx.enter_context(nc.psum_tensor("scores", [P, 1024], F32))
        probs_t = ctx.enter_context(nc.psum_tensor("probs_t", [P, 1024], F32))
        bank += [scores[:, 0:512], scores[:, 512:1024], probs_t[:, 0:512], probs_t[:, 512:1024]]

        x = sb("x", [P, KT, SEQ])
        hn_hi = sb("hn_hi", [P, KT, SEQ], F32R)
        hn_lo = sb("hn_lo", [P, KT, SEQ], F32R)
        raw = [sb(f"raw{i}", [P, UNIT]) for i in range(RAW)]
        w_hi = [sb(f"w_hi{i}", [P, UNIT], F32R) for i in range(4)]
        w_lo = [sb(f"w_lo{i}", [P, UNIT], F32R) for i in range(4)]
        atmp = [sb(f"atmp{i}", [P, HALF]) for i in range(2)]
        full = [sb(f"full{i}", [P, HALF]) for i in range(2)]
        acc = sb("acc", [P, HALF])
        rstd = [sb(f"rstd{h}", [P, HALF]) for h in range(NH2)]
        ones = sb("ones", [P, P])
        ident = sb("ident", [P, P])
        gain = sb("gain", [P, 5, KT])
        vgain = sb("vgain", [P, GMLP // P])
        eps = sb("eps", [P, 1])
        ssq = sb("ssq", [P, BLOCKS])
        ssq_part = sb("ssq_part", [P, BLOCKS])
        rv = sb("rv", [P, BLOCKS])
        rowmax = sb("rowmax", [P, 2])
        negmax = sb("negmax", [P, 2])
        rowsum = sb("rowsum", [P, 2])
        rowinv = sb("rowinv", [P, 2])

        with ExitStack() as a:
            y_hi = sb("y_hi", [P, 2, SEQ], F32R, a)
            y_lo = sb("y_lo", [P, 2, SEQ], F32R, a)
            v_raw = [sb(f"v_raw{i}", [P, 4, GDIM], F32, a) for i in range(NH2)]
            v_hi = sb("v_hi", [P, 4, GDIM], F32R, a)
            v_lo = sb("v_lo", [P, 4, GDIM], F32R, a)
            mixed = sb("mixed", [P, HALF], F32, a)
            ws_raw = sb("ws_raw", [P, P], F32, a)
            ws_hi = sb("ws_hi", [P, P], F32R, a)
            ws_lo = sb("ws_lo", [P, P], F32R, a)
            bs = sb("bs", [P, P], F32, a)
        with ExitStack() as f:
            w_hi += [sb(f"w_hi{i}", [P, UNIT], F32R, f) for i in (4, 5)]
            w_lo += [sb(f"w_lo{i}", [P, UNIT], F32R, f) for i in (4, 5)]
            h_hi = sb("h_hi", [P, 2, SEQ], F32R, f)
            h_lo = sb("h_lo", [P, 2, SEQ], F32R, f)
        q_hi = sb("q_hi", [P, SEQ], F32R)
        q_lo = sb("q_lo", [P, SEQ], F32R)
        k_hi = sb("k_hi", [P, SEQ], F32R)
        k_lo = sb("k_lo", [P, SEQ], F32R)
        vz_hi = sb("vz_hi", [P, BLOCKS, 2, P], F32R)
        vz_lo = sb("vz_lo", [P, BLOCKS, 2, P], F32R)
        bias = sb("bias", [P, 2, WIN])
        prob = [sb(f"prob{i}", [P, WIN]) for i in range(2)]
        pt_hi = [sb(f"pt_hi{i}", [P, WIN], F32R) for i in range(2)]
        pt_lo = [sb(f"pt_lo{i}", [P, WIN], F32R) for i in range(2)]
        o_hi = sb("o_hi", [P, HALF], F32R)
        o_lo = sb("o_lo", [P, HALF], F32R)
        rel = v_raw[0][0:HEADS, :, :].rearrange("p t n -> p (t n)")[:, 0:N_REL]
        rel_pad = v_raw[1][0:HEADS, :, :].rearrange("p t n -> p (t n)")[:, 0:REV]

        taken, step_begun = sem("taken"), sem("step_begun")
        small_in = sem("small_in")
        rel_in, rel_padded, rel_out = sem("rel_in"), sem("rel_padded"), sem("rel_out")
        x_in = [sem(f"x_in{h}") for h in range(NH2)]
        consts = sem("consts")
        raw_in = [sem(f"raw_in{i}") for i in range(RAW)]
        w_split = sem("w_split")
        v_used = sem("v_used")
        sq_done, acc_done, mean_done = sem("sq_done"), sem("acc_done"), sem("mean_done")
        std_done, rstd_done = sem("std_done"), sem("rstd_done")
        hn_full, hn_hi_done, hn_done = sem("hn_full"), sem("hn_hi_done"), sem("hn_done")
        v_done, v_gelu, v_ssq, v_sum = sem("v_done"), sem("v_gelu"), sem("v_ssq"), sem("v_sum")
        v_out = [sem(f"v_out{i}") for i in range(4)]
        rv_std, rv_done = sem("rv_std"), sem("rv_done")
        v_in = [sem(f"v_in{i}") for i in range(NH2)]
        ws_in, ws_masked, ws_hi_done, ws_lo_done = sem("ws_in"), sem("ws_masked"), sem("ws_hi_done"), sem("ws_lo_done")
        vs_hi, vs_lo = sem("vs_hi"), sem("vs_lo")
        mix_done = sem("mix_done")

        class Hidden:
            def __init__(self, name):
                self.mm = sem(name + "_mm")
                self.act = sem(name + "_act")
                self.full = sem(name + "_full")
                self.hi = sem(name + "_hi")
                self.lo = sem(name + "_lo")
                self.down = sem(name + "_down")
                self.added = sem(name + "_added")

        hid = {"G": Hidden("g"), "F1": Hidden("f1"), "F2": Hidden("f2")}

        p_done, p_read = sem("p_done"), sem("p_read")
        p_hi = sem("p_hi")
        qk_done, biased, neg_done, exp_done = sem("qk_done"), sem("biased"), sem("neg_done"), sem("exp_done")
        inv_done, normed, t_done = sem("inv_done"), sem("normed"), sem("t_done")
        pt_hi_done, pt_lo_done, pv_done = sem("pt_hi_done"), sem("pt_lo_done"), sem("pv_done")
        o_hi_done, o_lo_done = sem("o_hi_done"), sem("o_lo_done")
        bias_in, bias_masked, vz_zero = sem("bias_in"), sem("bias_masked"), sem("vz_zero")
        y_full = sem("y_full")
        y_out = [sem(f"y_out{i}") for i in range(2)]

        def r32(ap):
            return ap.bitcast(F32)

        def toks(h):
            return slice(h * HALF, (h + 1) * HALF)

        NORMS = ["load", "G", "F1", "B", "F2"]

        EARLY = [5, 5, 5, KT, 5]

        def x_final(eng, n, h, k):
            before = NORMS[n]
            if before == "load":
                eng.wait_ge(x_in[h], 16)
            elif before == "B":
                eng.wait_ge(p_read, p_number(PAIRS - 1, f"out{h}", k, True) + 1)
            else:
                its = GROUPS if before == "G" else CHUNKS
                eng.wait_ge(hid[before].added, 16 * (its - 1) + 8 * h + k + 1)

        def mean_bank(n, h):
            return bank[4 + h] if NORMS[n] in ("load", "B") else bank[4 * h]

        P_BODY = 24

        def p_number(it, what, i=0, last=False):
            if isinstance(it, int) and it < 0:
                return i
            at = {"k": 0, "v": 2, "vt": 4, "out0": 6, "q": 14, "out1": 14 if last else 16}[what] + i
            return it * P_BODY + (2 + at)

        def flipped(ap):
            return ap.rearrange("p (t c) -> p t c", c=P)[:, :, ::-1]

        def tiled(ap):
            return ap.rearrange("p (t c) -> p t c", c=P)

        def p_bank(it, what, i=0, last=False):
            return bank[p_number(min(it, 0) if isinstance(it, int) else 0, what, i, last) % 3]

        def in_heads(vz, h, view=lambda ap: ap):
            return view(vz[:, 4 * h:4 * h + 4, :, :]).rearrange("p t a (b c) -> p t (a b) c", c=HD)[:, :, 0::3, :]

        def by_head(ap):
            return ap[:, :].rearrange("p (t a c) -> p t a c", t=4, a=2)

        block = ctx.enter_context(nc.Block())


        @block.sync
        def _(sp):
            def unit(u, r, split):
                ge(sp, w_split, split)
                src = w_units[u] if isinstance(u, int) else w_units[bass.ds(u, 1), :, :].rearrange("u p n -> (u p) n")
                sp.dma_start(raw[r][:, :], src).then_inc(raw_in[r], 16)

            sp.dma_start(gain[:, :, :], gains).then_inc(small_in, 16)
            sp.dma_start(vgain[:, :], v_gain).then_inc(small_in, 16)
            sp.dma_start(ident[:, :], ident_d).then_inc(small_in, 16)
            sp.dma_start(rel, rel_rev).then_inc(rel_in, 16)
            for h in range(NH2):
                sp.dma_start(x[:, :, toks(h)], x_t[:, :, toks(h)].rearrange("k p n -> p k n")).then_inc(x_in[h], 16)
            for r in range(RAW):
                unit(r, r, 0)
            sp.wait_ge(rel_padded, 3)
            sp.dma_start(rel_scratch, rel_pad).then_inc(rel_out, 16)
            with sp.Fori(1, UNITS // RAW) as j:
                for r in range(RAW):
                    unit(j * RAW + r, r, j * (2 * RAW) + (2 * r - 2 * RAW + 2))
            for h in range(NH2):
                for k in range(KT):
                    sp.wait_ge(y_full, h * KT + k + 1)
                    sp.dma_start(out_t[k][:, toks(h)], full[k % 2][:, :]).then_inc(y_out[k % 2], 16)
            for i in range(2):
                sp.wait_ge(y_out[i], 16 * KT)

        @block.gpsimd
        def _(pool):
            def split(u, r, loads, slot):
                pool.wait_ge(raw_in[r], loads)
                pool.sem_inc(taken)
                pool.tensor_scalar(w_hi[slot][:, :], raw[r][:, :], 1.0, 1.0, ALU.mult, ALU.mult).then_inc(w_split, 1)
                pool.wait_ge(w_split, u * 2 + 1)
                pool.tensor_tensor(w_lo[slot][:, :], raw[r][:, :], r32(w_hi[slot][:, :]),
                                   ALU.subtract).then_inc(w_split, 1)

            def units(base, count, per, used):
                def one(it):
                    for s in range(per):
                        used(it, s)
                        split(it * per + (base + s), (base + s) % RAW,
                              it * (16 * per // RAW) + 16 * ((base + s) // RAW + 1), s)
                one(0)
                with pool.Fori(1, count) as it:
                    one(it)

            def used_v(it, s):
                if s < 3:
                    ge(pool, v_used, it * 3 + (s - 2))
                else:
                    ge(pool, v_done, it * 8)

            def used_g(it, s):
                if isinstance(it, int):
                    pool.wait_ge(v_done, CB * BLOCKS)
                elif s < 2:
                    pool.wait_ge(hid["G"].mm, it * 4 + (s - 1))
                else:
                    pool.wait_ge(hid["G"].down, it * 16)

            def used_f(name):
                def used(it, s):
                    if not isinstance(it, int):
                        if s < 4:
                            pool.wait_ge(hid[name].mm, it * 4 + (s // 2 - 1))
                        else:
                            pool.wait_ge(hid[name].down, it * 16)
                    elif name == "F1":
                        if s < 2:
                            pool.wait_ge(hid["G"].mm, 4 * GROUPS - 1 + s)
                        else:
                            pool.wait_ge(hid["G"].down, 16 * GROUPS)
                    else:
                        pool.wait_ge(p_done, [p_number(PAIRS - 2, "out1", 7), p_number(PAIRS - 1, "k", 1),
                                              p_number(PAIRS - 1, "v", 1)][s] + 1 if s < 3
                                     else p_number(PAIRS - 1, "out1", 7, True) + 1)
                return used

            def used_b(it, s):
                if isinstance(it, int):
                    pool.wait_ge(hid["F1"].mm, 4 * CHUNKS - 1 + s // 2)
                elif s == 0:
                    pool.wait_ge(p_done, it * P_BODY + (2 - 2 * P_BODY + 24))
                else:
                    before = {1: ("k", 1), 2: ("v", 1), 3: ("q", 1)}[s]
                    pool.wait_ge(p_done, it * P_BODY + (p_number(0, *before) + 1 - P_BODY))

            units(B_V, CB, 4, used_v)
            units(B_G, GROUPS, 4, used_g)
            units(B_F1, CHUNKS, 6, used_f("F1"))
            units(B_B, PAIRS, 4, used_b)
            units(B_F2, CHUNKS, 6, used_f("F2"))

        @block.tensor
        def _(pe):
            def product(out, lhs, rhs, start, stop, signal=None):
                (lh, ll), (rh, rl) = lhs, rhs
                pe.matmul(out, lh, rh, start=start, stop=False)
                pe.matmul(out, lh, rl, start=False, stop=False)
                last = pe.matmul(out, ll, rh, start=False, stop=stop)
                if signal is not None:
                    last.then_inc(signal, 1)

            def w(slot, lo, hi):
                return w_hi[slot][:, lo:hi], w_lo[slot][:, lo:hi]

            def hn(k, sl):
                return hn_hi[:, k, sl], hn_lo[:, k, sl]

            def project(out, slot, unit, h, norm, signal=None):
                pe.wait_ge(w_split, unit * 2 + 2)
                for k in range(KT):
                    pe.wait_ge(hn_done, 16 * norm + 8 * h + k + 1)
                    product(out, w(slot, k * P, (k + 1) * P), hn(k, toks(h)), k == 0, k == KT - 1,
                            signal if k == KT - 1 else None)

            def mean(n, h):
                pe.wait_ge(acc_done, 7 * (NH2 * n + h) + 7)
                pe.matmul(mean_bank(n, h)[:, :], ones[:, :], acc[:, :], start=True, stop=True).then_inc(mean_done, 1)

            def v_block(it, first, last):
                for th in range(NH2):
                    for j in range(4):
                        pe.wait_ge(w_split, it * 8 + (2 * j + 2))
                        for kk in range(2):
                            k = 2 * j + kk
                            pe.wait_ge(hn_done, 8 * th + k + 1)
                            for t in range(4 * th, 4 * th + 4):
                                if k == 0:
                                    ge(pe, v_gelu, it * 8 + (t - 7))
                                end = t == 4 * th + 3 and kk == 1 and th == 1 and j < 3
                                product(bank[t][:, :], hn(k, slice(t * P, (t + 1) * P)), w(j, kk * 512, kk * 512 + 512),
                                        k == 0, k == KT - 1, v_done if k == KT - 1 else v_used if end else None)

            def hidden(name, u0, per, it, first, last, norm, event, hi, lo):
                s = hid[name]
                for j in range(4):
                    h, f = divmod(j, 2)
                    ge(pe, s.full, it * 4 + (j - 1))
                    event(it, h, f, s)
                    if first and j == 0:
                        mean(norm, 1)
                for h in range(NH2):
                    pe.wait_ge(v_gelu, CB * BLOCKS)
                    pe.wait_ge(s.lo, it * 4 + (2 * h + 2))
                    for n in range(KT):
                        d = 8 * h + n
                        ge(pe, s.added, it * 16 + (d - 3))
                        for f in range(2):
                            slot = per - 2 + f
                            if h == 0 and n == 0:
                                pe.wait_ge(w_split, (it * per + (u0 + slot)) * 2 + 2)
                            product(bank[4 + d % 4][:, :], w(slot, n * P, (n + 1) * P),
                                    (hi[:, f, toks(h)], lo[:, f, toks(h)]), f == 0, f == 1, s.down if f == 1 else None)
                        if last and h == 1 and n == 2:
                            mean(norm + 1, 0)

            def gmlp_event(it, h, f, s):
                pe.wait_ge(v_gelu, (CB - 1) * BLOCKS + 2 * f + 2)
                project(bank[2 * f + 1][:, :], f, it * 4 + (B_G + f), h, 0)
                pe.wait_ge(vs_lo, it * 8 + (4 * h + 4))
                pe.wait_ge(ws_lo_done, it + 1)
                ch = slice(f * P, (f + 1) * P)
                for t in range(4):
                    product(bank[2 * f][:, t * P:(t + 1) * P], (v_hi[:, t, ch], v_lo[:, t, ch]),
                            (ws_hi[:, :], ws_lo[:, :]), True, True, s.mm if t == 3 else None)

            def ffn_event(u0, norm):
                def event(it, h, f, s):
                    project(bank[2 * f][:, :], 2 * f, it * 6 + (u0 + 2 * f), h, norm)
                    project(bank[2 * f + 1][:, :], 2 * f + 1, it * 6 + (u0 + 2 * f + 1), h, norm, s.mm)
                return event

            def fill(it, what, i=0, last=False):
                ge(pe, p_read, p_number(it, what, i, last) - 2)
                return p_bank(it, what, i, last)

            def query_product(it, h, unit, slot):
                ge(pe, p_read, p_number(it, "q", h) - 2)
                project(p_bank(it, "q", h)[:, :], slot, unit, h, 2, p_done)

            def out_product(it, h, n, last, slot):
                out = fill(it, f"out{h}", n, last)
                product(out[:, :], w(slot, n * P, (n + 1) * P), (o_hi[:, :], o_lo[:, :]), True, True, p_done)

            def scores_of(it, s):
                i, head = divmod(s, 2)
                rows = slice(head * HD, (head + 1) * HD)
                if s == 0:
                    pe.wait_ge(p_read, p_number(it, "k", 1) + 1)
                ge(pe, biased, it * 16 + s)
                off = max(0, LEFT - i) * P
                tq = slice(i * P, (i + 1) * P)
                parts = ([(off, LEFT * P)] if off < LEFT * P else []) + [(LEFT * P, WIN)]
                for at, to in parts:
                    tk = slice((i - LEFT) * P + at, (i - LEFT) * P + to)
                    product(scores[:, at:to], (q_hi[rows, tq], q_lo[rows, tq]), (k_hi[rows, tk], k_lo[rows, tk]),
                            True, True, qk_done if to == WIN else None)

            def transpose_probs(it, s):
                i = s // 2
                pe.wait_ge(normed, it * 16 + (s + 1))
                ge(pe, pt_lo_done, it * 16 + s)
                for j in range(max(0, LEFT - i), LEFT + 1):
                    t = pe.transpose(probs_t[:, j * P:(j + 1) * P], prob[s % 2][:, j * P:(j + 1) * P], ident[:, :])
                t.then_inc(t_done, 1)

            def values(it, s):
                i, head = divmod(s, 2)
                pe.wait_ge(p_read, p_number(it, "vt", i // 4) + 1)
                pe.wait_ge(pt_lo_done, it * 16 + (s + 1))
                if s % 8 == 0:
                    ge(pe, o_lo_done, it * 2 + i // 4)
                first = max(0, LEFT - i)
                for j in range(first, LEFT + 1):
                    key = i - LEFT + j
                    at = slice(j * P, (j + 1) * P)
                    product(bank[3][:, (i % 4) * P:(i % 4 + 1) * P], (vz_hi[:, key, head, :], vz_lo[:, key, head, :]),
                            (pt_hi[s % 2][:, at], pt_lo[s % 2][:, at]), head == 0 and j == first,
                            head == 1 and j == LEFT, pv_done if j == LEFT else None)

            def attention(it, first, last):
                u = it * 4 + B_B
                if first:
                    query_product(-1, 0, B_B, 0)
                    mean(2, 1)
                    query_product(-1, 1, B_B, 0)
                for h in range(NH2):
                    project(fill(it, "k", h)[:, :], 1, u + 1, h, 2, p_done)
                for m in range(19):
                    if m < 16:
                        scores_of(it, m)
                    if m < 2:
                        project(fill(it, "v", m)[:, :], 2, u + 2, m, 2, p_done)
                    if m == 2:
                        for h in range(NH2):
                            pe.wait_ge(p_read, p_number(it, "v", h) + 1)
                            out = fill(it, "vt", h)
                            for t in range(4):
                                tr = pe.transpose(out[:, t * P:(t + 1) * P], atmp[h][:, t * P:(t + 1) * P], ident[:, :])
                            tr.then_inc(p_done, 1)
                    if 0 <= m - 2 < 16:
                        transpose_probs(it, m - 2)
                    if 0 <= m - 3 < 16:
                        values(it, m - 3)
                    if m >= 11:
                        if m == 11:
                            pe.wait_ge(w_split, (u + (3 if last else 4)) * 2 + 2)
                            pe.wait_ge(o_lo_done, it * 2 + 1)
                        out_product(it, 0, m - 11, last, 3 if last else 0)
                if not last:
                    for h in range(NH2):
                        query_product(it, h, u + 3, 3)
                pe.wait_ge(o_lo_done, it * 2 + 2)
                for n in range(KT):
                    out_product(it, 1, n, last, 3 if last else 0)
                    if last and n == 2:
                        mean(3, 0)

            pe.wait_ge(small_in, 48)
            pe.wait_ge(consts, 1)
            mean(0, 0)
            mean(0, 1)
            repeat(pe, CB, v_block)
            def gmlp(it, first, last):
                hidden("G", B_G, 4, it, False, last, 0, gmlp_event, y_hi, y_lo)
            repeat(pe, GROUPS, gmlp)
            def ffn1(it, first, last):
                hidden("F1", B_F1, 6, it, first, last, 1, ffn_event(B_F1, 1), h_hi, h_lo)
            repeat(pe, CHUNKS, ffn1)
            repeat(pe, PAIRS, attention)
            pe.wait_ge(p_read, p_number(PAIRS - 1, "out1", 7, True) + 1)
            def ffn2(it, first, last):
                hidden("F2", B_F2, 6, it, first, last, 3, ffn_event(B_F2, 3), h_hi, h_lo)
            repeat(pe, CHUNKS, ffn2)
            mean(4, 1)

        @block.scalar
        def _(act):
            def square(n, h, k):
                x_final(act, n, h, k)
                halves = NH2 * n + h
                if k == 0:
                    ge(act, mean_done, halves)
                    dst = acc
                else:
                    ge(act, acc_done, 7 * halves + max(0, k - 2))
                    dst = atmp[k % 2]
                act.activation(dst[:, :], x[:, k, toks(h)], ACT.Square).then_inc(sq_done, 1)

            def std(n, h):
                act.wait_ge(mean_done, NH2 * n + h + 1)
                act.activation(rstd[h][:, :], mean_bank(n, h)[:, :], ACT.Sqrt, bias=eps[:, 0:1]).then_inc(std_done, 1)

            def norm(n, h0_squares=True):
                for k in range(KT if h0_squares else 0):
                    square(n, 0, k)
                for k in range(EARLY[n]):
                    square(n, 1, k)
                std(n, 0)
                hi(n, 0)
                for k in range(EARLY[n], KT):
                    square(n, 1, k)
                std(n, 1)
                hi(n, 1)

            def hi(n, h):
                for k in range(KT if n < 4 else 0):
                    act.wait_ge(hn_full, 16 * n + 8 * h + k + 1)
                    act.activation(hn_hi[:, k, toks(h)], full[k % 2][:, :], ACT.Copy).then_inc(hn_hi_done, 1)

            vst = [atmp[0], atmp[1], full[0], full[1]]

            def v_block(it, first, last):
                for t in range(BLOCKS):
                    r = t % 4
                    act.wait_ge(v_done, it * 8 + (t + 1))
                    ge(act, v_ssq, it * 8 + (t - 3))
                    if not (first and t < 4):
                        act.wait_ge(v_out[r], it * 32 + 16 * (t // 4))
                    act.activation(vst[r][:, :], bank[t][:, :], ACT.Gelu_apprx_tanh).then_inc(v_gelu, 1)
                    act.wait_ge(v_gelu, it * 8 + (t + 1))
                    dst = v_scratch[t][:, it * 512:(it + 1) * 512] if isinstance(it, int) \
                        else v_scratch[t][:, bass.ds(it * 512, 512)]
                    act.dma_start(dst, vst[r][:, :]).then_inc(v_out[r], 16)

            def load_v(g, h):
                cols = slice(g * GDIM, (g + 1) * GDIM) if isinstance(g, int) else bass.ds(g * GDIM, GDIM)
                act.dma_start(v_raw[h][:, :, :], v_scratch[4 * h:4 * h + 4, :, cols].rearrange("t p n -> p t n")
                              ).then_inc(v_in[h], 16)

            def load_ws(g):
                if isinstance(g, int):
                    w_src, b_src = w_s_t[g], b_s[g:g + 1, :]
                else:
                    w_src = w_s_t[bass.ds(g, 1), :, :].rearrange("g q p -> (g q) p")
                    b_src = b_s[bass.ds(g, 1), :]
                act.dma_start(ws_raw[:, :], w_src).then_inc(ws_in, 16)
                act.dma_start(bs[:, :], b_src.broadcast_to([P, P])).then_inc(ws_in, 16)

            def hi_of_event(s, it, j, dst):
                act.wait_ge(s.full, it * 4 + (j + 1))
                h, f = divmod(j, 2)
                act.activation(dst[:, f, toks(h)], full[f][:, :], ACT.Copy).then_inc(s.hi, 1)

            def gmlp(it, first, last):
                s = hid["G"]
                act.wait_ge(ws_masked, it + 1)
                ge(act, s.mm, it * 4)
                act.activation(ws_hi[:, :], ws_raw[:, :], ACT.Copy).then_inc(ws_hi_done, 1)
                for j in range(4):
                    h, f = divmod(j, 2)
                    if f == 0:
                        act.wait_ge(v_in[h], (it + 1) * 16)
                        ge(act, s.mm, it * 4 + 2 * h)
                        for t in range(4):
                            act.activation(v_hi[:, t, :], v_raw[h][:, t, :], ACT.Copy,
                                           scale=rv[:, 4 * h + t:4 * h + t + 1]).then_inc(vs_hi, 1)
                    act.wait_ge(s.mm, it * 4 + (j + 1))
                    act.activation(atmp[f][:, :], bank[2 * f + 1][:, :], ACT.Gelu_apprx_tanh).then_inc(s.act, 1)
                    hi_of_event(s, it, j, y_hi)
                if not last:
                    act.wait_ge(vs_lo, (it + 1) * 8)
                    for h in range(NH2):
                        load_v(it + 1, h)
                    act.wait_ge(ws_lo_done, it + 1)
                    load_ws(it + 1)
                else:
                    norm(1)

            def ffn(name, n):
                def one(it, first, last):
                    s = hid[name]
                    for j in range(4):
                        f = j % 2
                        act.wait_ge(s.mm, it * 4 + (j + 1))
                        act.activation(atmp[f][:, :], bank[2 * f][:, :], ACT.Silu).then_inc(s.act, 1)
                        hi_of_event(s, it, j, h_hi)
                    if last:
                        norm(n)
                return one

            def load_bias(pair):
                act.dma_start(bias[:, :, :], bass.AP(rel_scratch_t, pair * (2 * REV), [[1, P], [REV, 2], [1, WIN]])
                              ).then_inc(bias_in, 16)

            def p_hi_part(it, what, i, dst, src=None, scale=1.0):
                act.wait_ge(p_done, p_number(it, what, i) + 1)
                act.activation(dst, src if src is not None else p_bank(it, what, i)[:, :], ACT.Copy,
                               scale=scale).then_inc(p_hi, 1)

            def attention(it, first, last):
                if first:
                    load_bias(0)
                    for h in range(NH2):
                        p_hi_part(-1, "q", h, flipped(q_hi[:, toks(h)]), tiled(p_bank(-1, "q", h)[:, :]), HD ** -0.5)
                for h in range(NH2):
                    p_hi_part(it, "k", h, k_hi[:, toks(h)])
                for m in range(19):
                    if m == 2:
                        for h in range(NH2):
                            p_hi_part(it, "vt", h, in_heads(vz_hi, h), by_head(p_bank(it, "vt", h)))
                    if 0 <= m - 2 < 16:
                        s = m - 2
                        off = max(0, LEFT - s // 2) * P
                        act.wait_ge(t_done, it * 16 + (s + 1))
                        ge(act, pv_done, it * 16 + (s - 1))
                        act.activation(pt_hi[s % 2][:, off:], probs_t[:, off:WIN], ACT.Copy).then_inc(pt_hi_done, 1)
                    if m < 16:
                        off = max(0, LEFT - m // 2) * P
                        act.wait_ge(neg_done, it * 16 + (m + 1))
                        act.activation(prob[m % 2][:, off:], prob[m % 2][:, off:], ACT.Exp,
                                       bias=negmax[:, m % 2:m % 2 + 1],
                                       accum_out=rowsum[:, m % 2:m % 2 + 1]).then_inc(exp_done, 1)
                    if m == 15 and not last:
                        load_bias(it + 1)
                    if m in (10, 18):
                        act.wait_ge(pv_done, it * 16 + (8 if m == 10 else 16))
                        if m == 18:
                            act.wait_ge(p_done, p_number(it, "out0", 7) + 1)
                        act.activation(flipped(o_hi[:, :]), tiled(bank[3][:, :]), ACT.Copy).then_inc(o_hi_done, 1)
                if not last:
                    for h in range(NH2):
                        p_hi_part(it, "q", h, flipped(q_hi[:, toks(h)]), tiled(p_bank(it, "q", h)[:, :]), HD ** -0.5)
                else:
                    norm(3)

            act.wait_ge(consts, 1)
            norm(0)
            act.wait_ge(hn_done, 16)
            repeat(act, CB, v_block)
            act.wait_ge(v_sum, CB)
            act.activation(rv[:, :], ssq[:, :], ACT.Sqrt, bias=eps[:, 0:1], scale=1.0 / GMLP).then_inc(rv_std, 1)
            for r in range(4):
                act.wait_ge(v_out[r], 2 * CB * 16)
            act.wait_ge(rel_out, 16)
            for h in range(NH2):
                load_v(0, h)
            load_ws(0)
            act.wait_ge(rv_done, 1)
            repeat(act, GROUPS, gmlp)
            repeat(act, CHUNKS, ffn("F1", 2))
            repeat(act, PAIRS, attention)
            repeat(act, CHUNKS, ffn("F2", 4))

        @block.vector
        def _(dve):
            def add_squares(n, h, k):
                base = 7 * (NH2 * n + h)
                dve.wait_ge(sq_done, 8 * (NH2 * n + h) + k + 1)
                ge(dve, acc_done, base + k - 1)
                dve.tensor_tensor(acc[:, :], acc[:, :], atmp[k % 2][:, :], ALU.add).then_inc(acc_done, 1)

            def inverse(n, h):
                dve.wait_ge(std_done, NH2 * n + h + 1)
                dve.reciprocal(rstd[h][:, :], rstd[h][:, :]).then_inc(rstd_done, 1)
                dve.wait_ge(rstd_done, NH2 * n + h + 1)

            def normed_tile(n, h, k):
                e = 16 * n + 8 * h + k
                if n < 4:
                    if h or k >= 2:
                        dve.wait_ge(hn_done, e - 1)
                    dve.scalar_tensor_tensor(full[k % 2][:, :], x[:, k, toks(h)], gain[:, n, k:k + 1],
                                             rstd[h][:, :], ALU.mult, ALU.mult).then_inc(hn_full, 1)
                    dve.wait_ge(hn_hi_done, e + 1)
                    dve.tensor_tensor(hn_lo[:, k, toks(h)], full[k % 2][:, :], r32(hn_hi[:, k, toks(h)]),
                                      ALU.subtract).then_inc(hn_done, 1)
                else:
                    ge(dve, y_out[k % 2], 16 * (4 * h + k // 2))
                    dve.scalar_tensor_tensor(full[k % 2][:, :], x[:, k, toks(h)], gain[:, n, k:k + 1],
                                             rstd[h][:, :], ALU.mult, ALU.mult).then_inc(y_full, 1)

            def norm(n, add=lambda h, k: None, h0_added=False):
                for k in range(KT):
                    if not h0_added:
                        add(0, k)
                    if k:
                        add_squares(n, 0, k)
                for k in range(EARLY[n]):
                    add(1, k)
                    if k:
                        add_squares(n, 1, k)
                inverse(n, 0)
                for k in range(KT):
                    normed_tile(n, 0, k)
                for k in range(EARLY[n], KT):
                    add(1, k)
                    add_squares(n, 1, k)
                inverse(n, 1)
                for k in range(KT):
                    normed_tile(n, 1, k)

            vst = [atmp[0], atmp[1], full[0], full[1]]

            def v_block(it, first, last):
                for t in range(BLOCKS):
                    dve.wait_ge(v_gelu, it * 8 + (t + 1))
                    ge(dve, v_ssq, it * 8 + t)
                    if t == 0:
                        ge(dve, v_sum, it * 1)
                    dve.tensor_tensor_reduce(mixed[:, :], vst[t % 4][:, :], vst[t % 4][:, :], 1.0, 0.0, ALU.mult,
                                             ALU.add, ssq_part[:, t:t + 1]).then_inc(v_ssq, 1)
                dve.wait_ge(v_ssq, it * 8 + 8)
                dve.tensor_tensor(ssq[:, :], ssq[:, :], ssq_part[:, :], ALU.add).then_inc(v_sum, 1)

            def split_product(s, it, j, lo, hi_part, in1, up):
                h, f = divmod(j, 2)
                ge(dve, s.lo, it * 4 + (j - 1))
                dve.tensor_tensor(full[f][:, :], up, in1, ALU.mult).then_inc(s.full, 1)
                dve.wait_ge(s.hi, it * 4 + (j + 1))
                dve.tensor_tensor(lo[:, f, toks(h)], full[f][:, :], r32(hi_part[:, f, toks(h)]),
                                  ALU.subtract).then_inc(s.lo, 1)

            def adds(s, it):
                def add(h, n):
                    d = 8 * h + n
                    dve.wait_ge(s.down, it * 16 + (d + 1))
                    dve.tensor_tensor(x[:, n, toks(h)], bank[4 + d % 4][:, :], x[:, n, toks(h)],
                                      ALU.add).then_inc(s.added, 1)
                return add

            def all_adds(s, it, last, n):
                add = adds(s, it)
                if last:
                    norm(n, add)
                else:
                    for h in range(NH2):
                        for k in range(KT):
                            add(h, k)

            def gmlp(it, first, last):
                s = hid["G"]
                dve.wait_ge(ws_in, (it + 1) * 32)
                dve.memset(ws_raw[CHUNK:P, 0:CHUNK], 0.0).then_inc(ws_masked, 1)
                dve.wait_ge(ws_hi_done, it + 1)
                dve.tensor_tensor(ws_lo[:, :], ws_raw[:, :], r32(ws_hi[:, :]), ALU.subtract).then_inc(ws_lo_done, 1)
                for j in range(4):
                    h, f = divmod(j, 2)
                    if f == 0:
                        for t in range(4):
                            dve.wait_ge(vs_hi, it * 8 + (4 * h + t + 1))
                            dve.scalar_tensor_tensor(v_lo[:, t, :], v_raw[h][:, t, :], rv[:, 4 * h + t:4 * h + t + 1],
                                                     r32(v_hi[:, t, :]), ALU.mult, ALU.subtract).then_inc(vs_lo, 1)
                    dve.wait_ge(s.mm, it * 4 + (j + 1))
                    ge(dve, s.full, it * 4 + j)
                    g_col = vgain[:, 2 * it + f:2 * it + f + 1] if isinstance(it, int) else vgain[:, bass.ds(it * 2 + f, 1)]
                    dve.scalar_tensor_tensor(tiled(mixed[:, :]), tiled(bank[2 * f][:, :]), g_col,
                                             bs[:, None, :].broadcast_to([P, 4, P]), ALU.mult, ALU.add).then_inc(mix_done, 1)
                    dve.wait_ge(mix_done, it * 4 + (j + 1))
                    dve.wait_ge(s.act, it * 4 + (j + 1))
                    split_product(s, it, j, y_lo, y_hi, atmp[f][:, :], mixed[:, :])
                all_adds(s, it, last, 1)

            def ffn(name, n):
                def one(it, first, last):
                    s = hid[name]
                    for j in range(4):
                        f = j % 2
                        dve.wait_ge(s.act, it * 4 + (j + 1))
                        split_product(s, it, j, h_lo, h_hi, atmp[f][:, :], bank[2 * f + 1][:, :])
                    all_adds(s, it, last, n)
                return one

            def p_lo_part(it, what, i, number, dst, hi_part, src=None):
                src = src if src is not None else p_bank(it, what, i)[:, :]
                dve.wait_ge(p_hi, it * 6 + (2 + number))
                dve.tensor_tensor(dst, src, hi_part, ALU.subtract).then_inc(p_read, 1)

            def query_lo(it, h):
                dve.wait_ge(p_hi, it * 6 + (2 + 5 + h))
                dve.scalar_tensor_tensor(flipped(q_lo[:, toks(h)]), tiled(p_bank(it, "q", h)[:, :]), HD ** -0.5,
                                         flipped(r32(q_hi[:, toks(h)])), ALU.mult, ALU.subtract).then_inc(p_read, 1)

            def mask_bias(it):
                dve.wait_ge(bias_in, (it + 1) * 16)
                dve.memset(bias[CHUNK:P, :, WIN - CHUNK:WIN], MASKED).then_inc(bias_masked, 1)
                dve.memset(bias[0:CHUNK, :, 0:CHUNK], MASKED).then_inc(bias_masked, 1)

            def attention(it, first, last):
                def out_add(h, n):
                    dve.wait_ge(p_done, p_number(it, f"out{h}", n, last) + 1)
                    dve.tensor_tensor(x[:, n, toks(h)], p_bank(it, f"out{h}", n, last)[:, :], x[:, n, toks(h)],
                                      ALU.add).then_inc(p_read, 1)

                if first:
                    for part in (vz_hi, vz_lo):
                        for head in range(2):
                            dve.memset(r32(part[:, :, head, (1 - head) * HD:(2 - head) * HD]), 0.0).then_inc(vz_zero, 1)
                    for h in range(NH2):
                        query_lo(-1, h)
                    mask_bias(0)
                for h in range(NH2):
                    p_lo_part(it, "k", h, 1 + h, k_lo[:, toks(h)], r32(k_hi[:, toks(h)]))
                for m in range(19):
                    if m < 16:
                        off = max(0, LEFT - m // 2) * P
                        c = slice(m % 2, m % 2 + 1)
                        dve.wait_ge(qk_done, it * 16 + (m + 1))
                        if m == 0:
                            dve.wait_ge(bias_masked, it * 2 + 2)
                        ge(dve, t_done, it * 16 + (m - 1))
                        dve.sem_inc(step_begun)
                        dve.tensor_tensor_reduce(prob[m % 2][:, off:], scores[:, off:WIN], bias[:, m % 2, off:],
                                                 1.0, -3.0e38, ALU.add, ALU.max, rowmax[:, c]).then_inc(biased, 1)
                        dve.wait_ge(biased, it * 16 + (m + 1))
                        dve.tensor_scalar(negmax[:, c], rowmax[:, c], -1.0, None, ALU.mult).then_inc(neg_done, 1)
                    if 0 <= m - 1 < 16:
                        s = m - 1
                        off = max(0, LEFT - s // 2) * P
                        c = slice(s % 2, s % 2 + 1)
                        dve.wait_ge(exp_done, it * 16 + (s + 1))
                        dve.reciprocal(rowinv[:, c], rowsum[:, c]).then_inc(inv_done, 1)
                        dve.wait_ge(inv_done, it * 16 + (s + 1))
                        dve.tensor_scalar(prob[s % 2][:, off:], prob[s % 2][:, off:], rowinv[:, c], None,
                                          ALU.mult).then_inc(normed, 1)
                    if m < 2:
                        dve.wait_ge(p_done, p_number(it, "v", m) + 1)
                        dve.tensor_copy(atmp[m][:, :], p_bank(it, "v", m)[:, :]).then_inc(p_read, 1)
                    if m == 2:
                        for h in range(NH2):
                            p_lo_part(it, "vt", h, 3 + h, in_heads(vz_lo, h), in_heads(vz_hi, h, r32),
                                      by_head(p_bank(it, "vt", h)))
                    if 0 <= m - 2 < 16:
                        s = m - 2
                        off = max(0, LEFT - s // 2) * P
                        dve.wait_ge(pt_hi_done, it * 16 + (s + 1))
                        dve.tensor_tensor(pt_lo[s % 2][:, off:], probs_t[:, off:WIN], r32(pt_hi[s % 2][:, off:]),
                                          ALU.subtract).then_inc(pt_lo_done, 1)
                    if m in (10, 18):
                        dve.wait_ge(o_hi_done, it * 2 + (1 if m == 10 else 2))
                        dve.tensor_tensor(flipped(o_lo[:, :]), tiled(bank[3][:, :]), flipped(r32(o_hi[:, :])),
                                          ALU.subtract).then_inc(o_lo_done, 1)
                    if m >= 11:
                        out_add(0, m - 11)
                if not last:
                    for h in range(NH2):
                        query_lo(it, h)
                    for n in range(KT):
                        out_add(1, n)
                    mask_bias(it + 1)
                else:
                    norm(3, out_add, h0_added=True)

            dve.memset(ones[:, :], 1.0 / D)
            dve.memset(eps[:, :], EPS)
            dve.memset(ssq[:, :], 0.0)
            dve.drain().then_inc(consts, 1)
            dve.wait_ge(rel_in, 16)
            lead = WIN - P - 1
            dve.tensor_copy(rel_pad[:, 0:lead], rel[:, 0:1].broadcast_to([HEADS, lead])).then_inc(rel_padded, 1)
            dve.tensor_copy(rel_pad[:, lead:lead + N_REL], rel).then_inc(rel_padded, 1)
            dve.tensor_copy(rel_pad[:, lead + N_REL:], rel[:, N_REL - 1:N_REL].broadcast_to([HEADS, REV - lead - N_REL])
                            ).then_inc(rel_padded, 1)
            dve.wait_ge(small_in, 48)
            norm(0)
            repeat(dve, CB, v_block)
            dve.wait_ge(rv_std, 1)
            dve.reciprocal(rv[:, :], rv[:, :]).then_inc(rv_done, 1)
            dve.wait_ge(rv_done, 1)
            repeat(dve, GROUPS, gmlp)
            repeat(dve, CHUNKS, ffn("F1", 2))
            repeat(dve, PAIRS, attention)
            repeat(dve, CHUNKS, ffn("F2", 4))


def kernel(x, norm_mix_g, norm_ffn_g, final_g, a_w_in, a_v_gain, a_w_s, a_b_s, a_w_out, b_w_qkv, b_rel_bias,
           b_w_out, ffn_w_gate, ffn_w_up, ffn_w_down):
    import numpy as np
    import concourse.bacc as bacc
    from concourse.bass_utils import run_bass_kernel_spmd

    def tile_of(w, n):
        return w[:, n * P:(n + 1) * P].reshape(KT, P, P).transpose(1, 0, 2).reshape(P, UNIT)

    def rows_of(w, n):
        return w[n * P:(n + 1) * P, :]

    a = [np.asarray(t) for t in (a_w_in, a_w_out, b_w_qkv, b_w_out, ffn_w_gate, ffn_w_up, ffn_w_down)]
    w_in, w_out, w_qkv, w_o = (t[0] for t in a[:4])
    gate, up, down = a[4:]
    units = np.empty((UNITS, P, UNIT), np.float32)
    at = 0

    def put(unit):
        nonlocal at
        units[at] = unit
        at += 1

    for cb in range(CB):
        for j in range(4):
            v = w_in[2 * j * P:(2 * j + 2) * P, GMLP + cb * 512:GMLP + (cb + 1) * 512]
            put(v.reshape(2, P, 512).transpose(1, 0, 2).reshape(P, UNIT))
    for g in range(GROUPS):
        put(tile_of(w_in, 2 * g)), put(tile_of(w_in, 2 * g + 1))
        put(rows_of(w_out, 2 * g)), put(rows_of(w_out, 2 * g + 1))

    def ffn(i):
        for c in range(CHUNKS):
            for f in (2 * c, 2 * c + 1):
                put(tile_of(gate[i], f)), put(tile_of(up[i], f))
            put(rows_of(down[i], 2 * c)), put(rows_of(down[i], 2 * c + 1))

    ffn(0)
    put(tile_of(w_qkv, 0))
    for pair in range(PAIRS):
        put(tile_of(w_qkv, KT + pair)), put(tile_of(w_qkv, 2 * KT + pair))
        if pair < PAIRS - 1:
            put(tile_of(w_qkv, pair + 1))
        put(rows_of(w_o, pair))
    ffn(1)

    g = np.stack([np.asarray(t) for t in (norm_mix_g[0], norm_ffn_g[0], norm_mix_g[1], norm_ffn_g[1], final_g)])
    arrays = {
        "x_t": np.asarray(x)[0].T.reshape(KT, P, SEQ),
        "gains": g.reshape(5, KT, P).transpose(2, 0, 1),
        "v_gain": np.asarray(a_v_gain)[0].reshape(GMLP // P, P).T,
        "w_s_t": np.asarray(a_w_s)[0].transpose(0, 2, 1),
        "b_s": np.asarray(a_b_s)[0],
        "rel_rev": np.asarray(b_rel_bias)[0][:, ::-1],
        "ident": np.eye(P, dtype=np.float32),
        "w_units": units,
    }
    arrays = {name: np.ascontiguousarray(t) for name, t in arrays.items()}
    nc = bacc.Bacc("TRN2", target_bir_lowering=False, num_devices=1)
    ins = [nc.dram_tensor(name + "_in", t.shape, F32, kind="ExternalInput").ap() for name, t in arrays.items()]
    out = nc.dram_tensor("out_t", (KT, P, SEQ), F32, kind="ExternalOutput").ap()
    trunk(nc, *ins, out)
    r = run_bass_kernel_spmd(nc, [{name + "_in": t for name, t in arrays.items()}], core_ids=[0])
    return np.ascontiguousarray(r.results[0]["out_t"].reshape(D, SEQ).T).reshape(1, SEQ, D)
```

```python
from contextlib import ExitStack

import concourse.bass as bass
from concourse import mybir

F32 = mybir.dt.float32
F32R = mybir.dt.float32r
ALU = mybir.AluOpType
ACT = mybir.ActivationFunctionType

P = 128
SEQ = 1024
D = 1024
KT = D // P
HALF = SEQ // 2
NH2 = SEQ // HALF
UNIT = 1024
CHUNK = 64
EPS = 1e-6

GMLP = 2 * D
GROUPS = 8
GDIM = GMLP // GROUPS
BLOCKS = SEQ // P
CB = GMLP // 512

HEADS = 16
HD = D // HEADS
PAIRS = HEADS // 2
LEFT = 8 * CHUNK // P
WIN = (LEFT + 1) * P
N_REL = 192
SHIFT = P
SPLIT = 512 - SHIFT
REV = WIN + P - 1
MASKED = -1e30

D_FF = 2816
CHUNKS = D_FF // (2 * P)

RAW = 2
RING = 6

U_V = CB * 4
U_G = GROUPS * 4
U_F = CHUNKS * 6
U_B = PAIRS * 4
B_V, B_G = 0, U_V
B_F1 = B_G + U_G
B_B = B_F1 + U_F
B_F2 = B_B + U_B
UNITS = B_F2 + U_F


def ge(eng, sem, value):
    if isinstance(value, int) and value <= 0:
        return
    eng.wait_ge(sem, value)


def repeat(eng, n, body):
    body(0, True, False)
    with eng.Fori(1, n - 1) as it:
        body(it, False, False)
    body(n - 1, False, True)


def trunk(nc, x_t, gains, v_gain, w_s_t, b_s, rel_rev, ident_d, w_units, out_t):
    v_scratch = nc.dram_tensor("v_scratch", [BLOCKS, P, GMLP], F32).ap()
    rel_scratch_t = nc.dram_tensor("rel_scratch", [HEADS, REV], F32)
    rel_scratch = rel_scratch_t.ap()

    with ExitStack() as ctx:
        def sb(name, shape, dt=F32, at=ctx):
            return at.enter_context(nc.sbuf_tensor(name, shape, dt))

        def sem(name):
            return ctx.enter_context(nc.semaphore(name))

        bank = [ctx.enter_context(nc.psum_tensor(f"bank{i}", [P, 512], F32)) for i in range(4)]
        scores = ctx.enter_context(nc.psum_tensor("scores", [P, 1024], F32))
        probs_t = ctx.enter_context(nc.psum_tensor("probs_t", [P, 1024], F32))
        bank += [scores[:, 0:512], scores[:, 512:1024], probs_t[:, 0:512], probs_t[:, 512:1024]]

        x = sb("x", [P, KT, SEQ])
        hn_hi = sb("hn_hi", [P, KT, SEQ], F32R)
        hn_lo = sb("hn_lo", [P, KT, SEQ], F32R)
        raw = [sb(f"raw{i}", [P, UNIT]) for i in range(RAW)]
        w_hi = [sb(f"w_hi{i}", [P, UNIT], F32R) for i in range(4)]
        w_lo = [sb(f"w_lo{i}", [P, UNIT], F32R) for i in range(4)]
        atmp = [sb(f"atmp{i}", [P, HALF]) for i in range(2)]
        full = [sb(f"full{i}", [P, HALF]) for i in range(2)]
        acc = sb("acc", [P, HALF])
        rstd = [sb(f"rstd{h}", [P, HALF]) for h in range(NH2)]
        ones = sb("ones", [P, P])
        ident = sb("ident", [P, P])
        gain = sb("gain", [P, 5, KT])
        vgain = sb("vgain", [P, GMLP // P])
        eps = sb("eps", [P, 1])
        ssq = sb("ssq", [P, BLOCKS])
        ssq_part = sb("ssq_part", [P, BLOCKS])
        rv = sb("rv", [P, BLOCKS])
        rowmax = sb("rowmax", [P, 2])
        negmax = sb("negmax", [P, 2])
        rowsum = sb("rowsum", [P, 2])
        rowinv = sb("rowinv", [P, 2])

        with ExitStack() as a:
            y_hi = sb("y_hi", [P, 2, SEQ], F32R, a)
            y_lo = sb("y_lo", [P, 2, SEQ], F32R, a)
            v_raw = [sb(f"v_raw{i}", [P, 4, GDIM], F32, a) for i in range(NH2)]
            v_hi = sb("v_hi", [P, 4, GDIM], F32R, a)
            v_lo = sb("v_lo", [P, 4, GDIM], F32R, a)
            mixed = sb("mixed", [P, HALF], F32, a)
            ws_raw = sb("ws_raw", [P, P], F32, a)
            ws_hi = sb("ws_hi", [P, P], F32R, a)
            ws_lo = sb("ws_lo", [P, P], F32R, a)
            bs = sb("bs", [P, P], F32, a)
        with ExitStack() as f:
            w_hi += [sb(f"w_hi{i}", [P, UNIT], F32R, f) for i in (4, 5)]
            w_lo += [sb(f"w_lo{i}", [P, UNIT], F32R, f) for i in (4, 5)]
            h_hi = sb("h_hi", [P, 2, SEQ], F32R, f)
            h_lo = sb("h_lo", [P, 2, SEQ], F32R, f)
        q_hi = sb("q_hi", [P, SEQ], F32R)
        q_lo = sb("q_lo", [P, SEQ], F32R)
        k_hi = sb("k_hi", [P, SEQ], F32R)
        k_lo = sb("k_lo", [P, SEQ], F32R)
        vz_hi = sb("vz_hi", [P, BLOCKS, 2, P], F32R)
        vz_lo = sb("vz_lo", [P, BLOCKS, 2, P], F32R)
        bias = sb("bias", [P, 2, WIN])
        prob = [sb(f"prob{i}", [P, WIN]) for i in range(2)]
        pt_hi = [sb(f"pt_hi{i}", [P, WIN], F32R) for i in range(2)]
        pt_lo = [sb(f"pt_lo{i}", [P, WIN], F32R) for i in range(2)]
        o_hi = sb("o_hi", [P, HALF], F32R)
        o_lo = sb("o_lo", [P, HALF], F32R)
        rel = v_raw[0][0:HEADS, :, :].rearrange("p t n -> p (t n)")[:, 0:N_REL]
        rel_pad = v_raw[1][0:HEADS, :, :].rearrange("p t n -> p (t n)")[:, 0:REV]

        taken, step_begun = sem("taken"), sem("step_begun")
        small_in = sem("small_in")
        rel_in, rel_padded, rel_out = sem("rel_in"), sem("rel_padded"), sem("rel_out")
        x_in = [[sem(f"x_in{h}_{k}") for k in range(KT)] for h in range(NH2)]
        consts = sem("consts")
        raw_in = [sem(f"raw_in{i}") for i in range(RAW)]
        w_split = sem("w_split")
        v_used = sem("v_used")
        sq_done, acc_done, mean_done = sem("sq_done"), sem("acc_done"), sem("mean_done")
        std_done, rstd_done = sem("std_done"), sem("rstd_done")
        hn_full, hn_hi_done, hn_done = sem("hn_full"), sem("hn_hi_done"), sem("hn_done")
        v_done, v_gelu, v_ssq, v_sum = sem("v_done"), sem("v_gelu"), sem("v_ssq"), sem("v_sum")
        v_out = [sem(f"v_out{i}") for i in range(4)]
        rv_std, rv_done = sem("rv_std"), sem("rv_done")
        v_in = [sem(f"v_in{i}") for i in range(NH2)]
        ws_in, ws_masked, ws_hi_done, ws_lo_done = sem("ws_in"), sem("ws_masked"), sem("ws_hi_done"), sem("ws_lo_done")
        vs_hi, vs_lo = sem("vs_hi"), sem("vs_lo")
        mix_done = sem("mix_done")

        class Hidden:
            def __init__(self, name):
                self.mm = sem(name + "_mm")
                self.act = sem(name + "_act")
                self.full = sem(name + "_full")
                self.hi = sem(name + "_hi")
                self.lo = sem(name + "_lo")
                self.down = sem(name + "_down")
                self.added = sem(name + "_added")

        hid = {"G": Hidden("g"), "F1": Hidden("f1"), "F2": Hidden("f2")}

        p_done, p_read = sem("p_done"), sem("p_read")
        p_hi = sem("p_hi")
        qk_done, biased, neg_done, exp_done = sem("qk_done"), sem("biased"), sem("neg_done"), sem("exp_done")
        inv_done, normed, t_done = sem("inv_done"), sem("normed"), sem("t_done")
        pt_hi_done, pt_lo_done, pv_done = sem("pt_hi_done"), sem("pt_lo_done"), sem("pv_done")
        o_hi_done, o_lo_done = sem("o_hi_done"), sem("o_lo_done")
        bias_in, bias_masked, vz_zero = sem("bias_in"), sem("bias_masked"), sem("vz_zero")
        y_full = sem("y_full")
        y_out = sem("y_out")

        def r32(ap):
            return ap.bitcast(F32)

        def toks(h):
            return slice(h * HALF, (h + 1) * HALF)

        NORMS = ["load", "G", "F1", "B", "F2"]

        def x_final(eng, n, h, k):
            before = NORMS[n]
            if before == "load":
                eng.wait_ge(x_in[h][k], 16)
            elif before == "B":
                eng.wait_ge(p_read, p_number(PAIRS - 1, f"out{h}", k) + 1)
            else:
                its = GROUPS if before == "G" else CHUNKS
                eng.wait_ge(hid[before].added, 16 * (its - 1) + 8 * h + k + 1)

        def mean_bank(n, h):
            return bank[4 + h] if NORMS[n] in ("load", "B") else bank[4 * h]

        def out_events(name, lo, hi):
            return [((name, n), n % 2) for n in range(lo, hi)]

        order = {-1: [(("q", 0), 2)]}
        for pair in range(PAIRS):
            order[pair] = [(("k", 0), 0), (("k", 1), 1), (("v", 0), 2), (("v", 1), 0), (("vt", 0), 1), (("vt", 1), 2)]
            if pair == 0:
                order[pair][:3] = [(("k", 0), 0), (("v", 0), 1), (("q first", 1), 2), (("k", 1), 1)]
            if pair:
                order[pair] += out_events("out1p", 0, KT)
            if pair < PAIRS - 1:
                order[pair] += out_events("out0", 0, 4) + [(("q", 0), 2)] + out_events("out0", 4, KT) + [(("q", 1), 2)]
            else:
                order[pair] += out_events("out0", 0, KT) + [(("out1", n), 2 + n % 2) for n in range(KT)]
        plan = [(pair, event, b) for pair in order for event, b in order[pair]]
        number = {(pair, event): n for n, (pair, event, b) in enumerate(plan)}
        before = {(pair, event): max([m for m in range(n) if plan[m][2] == b], default=-1)
                  for n, (pair, event, b) in enumerate(plan)}
        bank_of = {(pair, event): bank[b] for pair, event, b in plan}
        P_BODY = len(order[1])

        def by_pair(table, it, event):
            if isinstance(it, int):
                return table[it, event]
            assert all(table[pair, event] == table[1, event] + (pair - 1) * P_BODY for pair in range(1, PAIRS - 1))
            return it * P_BODY + (table[1, event] - P_BODY)

        def p_number(it, what, i=0):
            return by_pair(number, it, (what, i))

        def p_bank(it, what, i=0):
            return bank_of[it if isinstance(it, int) else 1, (what, i)]

        OUT1P = {2: (0,), 3: (1, 2), 4: (3, 4), 5: (5,), 6: (6,), 7: (7,)}

        def flipped(ap):
            return ap.rearrange("p (t c) -> p t c", c=P)[:, :, ::-1]

        def tiled(ap):
            return ap.rearrange("p (t c) -> p t c", c=P)

        def in_heads(vz, h, view=lambda ap: ap):
            return view(vz[:, 4 * h:4 * h + 4, :, :]).rearrange("p t a (b c) -> p t (a b) c", c=HD)[:, :, 0::3, :]

        def by_head(ap):
            return ap[:, :].rearrange("p (t a c) -> p t a c", t=4, a=2)

        block = ctx.enter_context(nc.Block())


        @block.sync
        def _(sp):
            def unit(u, r, split):
                ge(sp, w_split, split)
                src = w_units[u] if isinstance(u, int) else w_units[bass.ds(u, 1), :, :].rearrange("u p n -> (u p) n")
                sp.dma_start(raw[r][:, :], src).then_inc(raw_in[r], 16)

            def load_x(h):
                for k in range(KT):
                    sp.dma_start(x[:, k, toks(h)], x_t[k][:, toks(h)]).then_inc(x_in[h][k], 16)

            load_x(0)
            sp.dma_start(gain[:, :, :], gains).then_inc(small_in, 16)
            sp.dma_start(vgain[:, :], v_gain).then_inc(small_in, 16)
            sp.dma_start(ident[:, :], ident_d).then_inc(small_in, 16)
            sp.dma_start(rel, rel_rev).then_inc(rel_in, 16)
            for r in range(RAW):
                unit(r, r, 0)
            load_x(1)
            sp.wait_ge(rel_padded, 3)
            sp.dma_start(rel_scratch, rel_pad).then_inc(rel_out, 16)
            with sp.Fori(1, UNITS // RAW) as j:
                for r in range(RAW):
                    unit(j * RAW + r, r, j * (2 * RAW) + (2 * r - 2 * RAW + 2))
            for h in range(NH2):
                for k in range(KT):
                    sp.wait_ge(y_full, h * KT + k + 1)
                    sp.dma_start(out_t[k][:, toks(h)], x[:, k, toks(h)]).then_inc(y_out, 16)
            sp.wait_ge(y_out, 16 * NH2 * KT)

        @block.gpsimd
        def _(pool):
            def split(u, r, loads, slot):
                pool.wait_ge(raw_in[r], loads)
                pool.sem_inc(taken)
                pool.tensor_scalar(w_hi[slot][:, :], raw[r][:, :], 1.0, 1.0, ALU.mult, ALU.mult).then_inc(w_split, 1)
                pool.wait_ge(w_split, u * 2 + 1)
                pool.tensor_tensor(w_lo[slot][:, :], raw[r][:, :], r32(w_hi[slot][:, :]),
                                   ALU.subtract).then_inc(w_split, 1)

            def units(base, count, per, used, peeled=1):
                def one(it):
                    for s in range(per):
                        used(it, s)
                        split(it * per + (base + s), (base + s) % RAW,
                              it * (16 * per // RAW) + 16 * ((base + s) // RAW + 1), s)
                for it in range(peeled):
                    one(it)
                with pool.Fori(peeled, count) as it:
                    one(it)

            def used_v(it, s):
                if s < 3:
                    ge(pool, v_used, it * 3 + (s - 2))
                else:
                    ge(pool, v_done, it * 8)

            def used_g(it, s):
                if isinstance(it, int):
                    pool.wait_ge(v_done, CB * BLOCKS)
                elif s < 2:
                    pool.wait_ge(hid["G"].mm, it * 4 + (s - 1))
                else:
                    pool.wait_ge(hid["G"].down, it * 16)

            def used_f(name):
                def used(it, s):
                    if not isinstance(it, int):
                        if s < 4:
                            pool.wait_ge(hid[name].mm, it * 4 + (s // 2 - 1))
                        else:
                            pool.wait_ge(hid[name].down, it * 16)
                    elif name == "F1":
                        if s < 2:
                            pool.wait_ge(hid["G"].mm, 4 * GROUPS - 1 + s)
                        else:
                            pool.wait_ge(hid["G"].down, 16 * GROUPS)
                    else:
                        pool.wait_ge(p_done, p_number(PAIRS - 1, *[("out1p", 7), ("k", 1), ("v", 1), ("out1", 7)][min(s, 3)]) + 1)
                return used

            def used_b(it, s):
                if isinstance(it, int) and it == 0:
                    pool.wait_ge(hid["F1"].mm, 4 * CHUNKS - 1 + s // 2)
                elif isinstance(it, int):
                    last = [number[0, ("q first", 1)], number[0, ("k", 1)], number[0, ("v", 1)], number[0, ("q", 1)]][s]
                    pool.wait_ge(p_done, last + 1)
                else:
                    last = p_number(1, *[("out1p", 7), ("k", 1), ("v", 1), ("q", 1)][s])
                    pool.wait_ge(p_done, it * P_BODY + (last + 1 - 2 * P_BODY))

            units(B_V, CB, 4, used_v)
            units(B_G, GROUPS, 4, used_g)
            units(B_F1, CHUNKS, 6, used_f("F1"))
            units(B_B, PAIRS, 4, used_b, peeled=2)
            units(B_F2, CHUNKS, 6, used_f("F2"))

        @block.tensor
        def _(pe):
            def product(out, lhs, rhs, start, stop, signal=None):
                (lh, ll), (rh, rl) = lhs, rhs
                pe.matmul(out, lh, rh, start=start, stop=False)
                pe.matmul(out, lh, rl, start=False, stop=False)
                last = pe.matmul(out, ll, rh, start=False, stop=stop)
                if signal is not None:
                    last.then_inc(signal, 1)

            def w(slot, lo, hi):
                return w_hi[slot][:, lo:hi], w_lo[slot][:, lo:hi]

            def hn(k, sl):
                return hn_hi[:, k, sl], hn_lo[:, k, sl]

            def project(outs, slot, unit, h, norm, signal=None, hooks=(), each=False):
                pe.wait_ge(w_split, (unit + (len(outs) - 1)) * 2 + 2)
                for k in range(KT):
                    pe.wait_ge(hn_done, 16 * norm + 8 * h + k + 1)
                    for i, out in enumerate(outs):
                        product(out, w(slot + i, k * P, (k + 1) * P), hn(k, toks(h)), k == 0, k == KT - 1,
                                signal if k == KT - 1 and (each or i == len(outs) - 1) else None)
                    for at, hook in hooks:
                        if at == k:
                            hook()

            def mean(n, h):
                pe.wait_ge(acc_done, 7 * (NH2 * n + h) + 7)
                pe.matmul(mean_bank(n, h)[:, :], ones[:, :], acc[:, :], start=True, stop=True).then_inc(mean_done, 1)

            def v_block(it, first, last):
                for th in range(NH2):
                    for j in range(4):
                        if first and th == 0 and j == 2:
                            mean(0, 1)
                        pe.wait_ge(w_split, it * 8 + (2 * j + 2))
                        for kk in range(2):
                            k = 2 * j + kk
                            pe.wait_ge(hn_done, 8 * th + k + 1)
                            for t in range(4 * th, 4 * th + 4):
                                if k == 0:
                                    ge(pe, v_gelu, it * 8 + (t - 7))
                                end = t == 4 * th + 3 and kk == 1 and th == 1 and j < 3
                                product(bank[t][:, :], hn(k, slice(t * P, (t + 1) * P)), w(j, kk * 512, kk * 512 + 512),
                                        k == 0, k == KT - 1, v_done if k == KT - 1 else v_used if end else None)

            def hidden(name, u0, per, it, last, norm, event, hi, lo, hooks):
                s = hid[name]

                def make(j):
                    h, f = divmod(j, 2)
                    ge(pe, s.full, it * 4 + (j - 1))
                    event(it, h, f, s, hooks.get(j, ()))

                def down(h):
                    if name == "G":
                        pe.wait_ge(v_gelu, CB * BLOCKS)
                    pe.wait_ge(s.lo, it * 4 + (2 * h + 2))
                    for n in range(KT):
                        d = 8 * h + n
                        ge(pe, s.added, it * 16 + (d - 3))
                        for f in range(2):
                            slot = per - 2 + f
                            if h == 0 and n == 0:
                                pe.wait_ge(w_split, (it * per + (u0 + slot)) * 2 + 2)
                            product(bank[4 + d % 4][:, :], w(slot, n * P, (n + 1) * P),
                                    (hi[:, f, toks(h)], lo[:, f, toks(h)]), f == 0, f == 1, s.down if f == 1 else None)

                if not last:
                    for j in range(4):
                        make(j)
                    down(0)
                    down(1)
                else:
                    for j in range(3):
                        make(j)
                    down(0)

                    def mean_0():
                        pe.wait_ge(s.full, it * 4 + 3)
                        mean(norm + 1, 0)
                    hooks = {3: ((KT - 1 if name == "G" else 3, mean_0),)}
                    make(3)
                    down(1)

            def gmlp_event(it, h, f, s, hooks):
                pe.wait_ge(v_gelu, (CB - 1) * BLOCKS + 2 * f + 2)
                project([bank[2 * f + 1][:, :]], f, it * 4 + (B_G + f), h, 0, None, hooks)
                pe.wait_ge(vs_lo, it * 8 + (4 * h + 4))
                pe.wait_ge(ws_lo_done, it + 1)
                ch = slice(f * P, (f + 1) * P)
                for t in range(4):
                    product(bank[2 * f][:, t * P:(t + 1) * P], (v_hi[:, t, ch], v_lo[:, t, ch]),
                            (ws_hi[:, :], ws_lo[:, :]), True, True, s.mm if t == 3 else None)

            def ffn_event(u0, norm):
                def event(it, h, f, s, hooks):
                    project([bank[2 * f][:, :], bank[2 * f + 1][:, :]], 2 * f, it * 6 + (u0 + 2 * f), h, norm, s.mm, hooks)
                return event

            def fill(it, what, i=0):
                ge(pe, p_read, by_pair(before, it, (what, i)) + 1)
                return p_bank(it, what, i)

            def part(it, what, h, k, unit, slot):
                if k == 0:
                    fill(it, what, h)
                    pe.wait_ge(w_split, unit * 2 + 2)
                product(p_bank(it, what, h)[:, :], w(slot, k * P, (k + 1) * P), hn(k, toks(h)), k == 0, k == KT - 1,
                        p_done if k == KT - 1 else None)

            def out_product(it, name, n, slot):
                out = fill(it, name, n)
                if name == "out1p":
                    pe.wait_ge(o_lo_done, it * 2)
                product(out[:, :], w(slot, n * P, (n + 1) * P), (o_hi[:, :], o_lo[:, :]), True, True, p_done)

            def scores_of(it, s):
                i, head = divmod(s, 2)
                rows = slice(head * HD, (head + 1) * HD)
                if s == 0:
                    pe.wait_ge(p_read, p_number(it, "k", 1) + 1)
                ge(pe, biased, it * 16 + s)
                off = max(0, LEFT - i) * P
                tq = slice(i * P, (i + 1) * P)
                parts = ([(off, SPLIT)] if off < SPLIT else []) + [(max(off, SPLIT), WIN)]
                for at, to in parts:
                    tk = slice((i - LEFT) * P + at, (i - LEFT) * P + to)
                    product(scores[:, SHIFT + at:SHIFT + to], (q_hi[rows, tq], q_lo[rows, tq]), (k_hi[rows, tk], k_lo[rows, tk]),
                            True, True, qk_done if to == WIN else None)

            def transpose_probs(it, s):
                i = s // 2
                pe.wait_ge(normed, it * 16 + (s + 1))
                ge(pe, pt_lo_done, it * 16 + s)
                for j in range(max(0, LEFT - i), LEFT + 1):
                    t = pe.transpose(probs_t[:, j * P:(j + 1) * P], prob[s % 2][:, j * P:(j + 1) * P], ident[:, :])
                t.then_inc(t_done, 1)

            def values(it, s):
                i, head = divmod(s, 2)
                pe.wait_ge(p_read, p_number(it, "vt", i // 4) + 1)
                pe.wait_ge(pt_lo_done, it * 16 + (s + 1))
                if s % 8 == 0:
                    ge(pe, o_lo_done, it * 2 + i // 4)
                first = max(0, LEFT - i)
                for j in range(first, LEFT + 1):
                    key = i - LEFT + j
                    at = slice(j * P, (j + 1) * P)
                    product(bank[3][:, (i % 4) * P:(i % 4 + 1) * P], (vz_hi[:, key, head, :], vz_lo[:, key, head, :]),
                            (pt_hi[s % 2][:, at], pt_lo[s % 2][:, at]), head == 0 and j == first,
                            head == 1 and j == LEFT, pv_done if j == LEFT else None)

            def attention(it, first, last):
                u = it * 4 + B_B
                if first:
                    project([fill(-1, "q", 0)[:, :], fill(0, "k", 0)[:, :], fill(0, "v", 0)[:, :]], 0, u, 0, 2,
                            p_done, ((5, lambda: mean(2, 1)),), each=True)
                    project([fill(0, "q first", 1)[:, :], fill(0, "k", 1)[:, :]], 0, u, 1, 2, p_done, each=True)
                else:
                    for what, slot in (("k", 1), ("v", 2)):
                        for h in range(NH2 if what == "k" else 1):
                            for k in range(KT):
                                part(it, what, h, k, u + slot, slot)
                for m in range(19):
                    if 0 <= m - 2 < 16:
                        transpose_probs(it, m - 2)
                    if m < 16:
                        scores_of(it, m)
                    if m < 2:
                        for k in range(4 * m, 4 * m + 4):
                            part(it, "v", 1, k, u + 2, 2)
                    if m == 2:
                        for h in range(NH2):
                            pe.wait_ge(p_read, p_number(it, "v", h) + 1)
                            out = fill(it, "vt", h)
                            for t in range(4):
                                tr = pe.transpose(out[:, t * P:(t + 1) * P], atmp[h][:, t * P:(t + 1) * P], ident[:, :])
                            tr.then_inc(p_done, 1)
                    if 8 <= m < 16 and not last:
                        part(it, "q", 0, m - 8, u + 3, 3)
                    if 0 <= m - 3 < 16:
                        values(it, m - 3)
                    for n in OUT1P.get(m, ()) if not first else ():
                        out_product(it, "out1p", n, 0)
                    if m >= 11:
                        if m == 11:
                            pe.wait_ge(w_split, (u + (3 if last else 4)) * 2 + 2)
                            pe.wait_ge(o_lo_done, it * 2 + 1)
                        out_product(it, "out0", m - 11, 3 if last else 0)
                if not last:
                    for k in range(KT):
                        part(it, "q", 1, k, u + 3, 3)
                    return
                pe.wait_ge(o_lo_done, it * 2 + 2)
                for n in range(KT):
                    out_product(it, "out1", n, 3)
                    if n == 1:
                        mean(3, 0)

            pe.wait_ge(small_in, 48)
            pe.wait_ge(consts, 1)
            mean(0, 0)
            repeat(pe, CB, v_block)
            def gmlp(it, first, last):
                hidden("G", B_G, 4, it, last, 0, gmlp_event, y_hi, y_lo, {})
            repeat(pe, GROUPS, gmlp)
            def ffn1(it, first, last):
                hooks = {0: ((KT - 1, lambda: mean(1, 1)),)} if first else {}
                hidden("F1", B_F1, 6, it, last, 1, ffn_event(B_F1, 1), h_hi, h_lo, hooks)
            repeat(pe, CHUNKS, ffn1)
            repeat(pe, PAIRS, attention)
            pe.wait_ge(p_read, p_number(PAIRS - 1, "out0", 7) + 1)
            def ffn2(it, first, last):
                def hook():
                    mean(3, 1)
                def banks_free():
                    pe.wait_ge(p_read, p_number(PAIRS - 1, "out1", 7) + 1)
                hooks = {0: ((KT - 1, banks_free),), 1: ((2, hook),)} if first else {}
                hidden("F2", B_F2, 6, it, last, 3, ffn_event(B_F2, 3), h_hi, h_lo, hooks)
            repeat(pe, CHUNKS, ffn2)
            mean(4, 1)

        @block.scalar
        def _(act):
            def square(n, h, k):
                x_final(act, n, h, k)
                halves = NH2 * n + h
                if k == 0:
                    ge(act, mean_done, halves)
                    dst = acc
                else:
                    ge(act, acc_done, 7 * halves + max(0, k - 2))
                    dst = atmp[k % 2]
                act.activation(dst[:, :], x[:, k, toks(h)], ACT.Square).then_inc(sq_done, 1)

            def std(n, h):
                act.wait_ge(mean_done, NH2 * n + h + 1)
                act.activation(rstd[h][:, :], mean_bank(n, h)[:, :], ACT.Sqrt, bias=eps[:, 0:1]).then_inc(std_done, 1)

            def squares(n, h, lo=0):
                for k in range(lo, KT):
                    square(n, h, k)

            def hi_tiles(n, h, lo=0, hi=KT):
                for k in range(lo, hi if n < 4 else 0):
                    act.wait_ge(hn_full, 16 * n + 8 * h + k + 1)
                    act.activation(hn_hi[:, k, toks(h)], full[k % 2][:, :], ACT.Copy).then_inc(hn_hi_done, 1)

            def last_half(n, event_3):
                squares(n, 0)
                if n == 1:
                    event_3()
                std(n, 0)
                if n > 1:
                    event_3()
                hi_tiles(n, 0)
                squares(n, 1)
                std(n, 1)

            vst = [atmp[0], atmp[1], full[0], full[1]]

            def v_block(it, first, last):
                for t in range(BLOCKS):
                    r = t % 4
                    act.wait_ge(v_done, it * 8 + (t + 1))
                    ge(act, v_ssq, it * 8 + (t - 3))
                    if not (first and t < 4):
                        act.wait_ge(v_out[r], it * 32 + 16 * (t // 4))
                    act.activation(vst[r][:, :], bank[t][:, :], ACT.Gelu_apprx_tanh).then_inc(v_gelu, 1)
                    act.wait_ge(v_gelu, it * 8 + (t + 1))
                    dst = v_scratch[t][:, it * 512:(it + 1) * 512] if isinstance(it, int) \
                        else v_scratch[t][:, bass.ds(it * 512, 512)]
                    act.dma_start(dst, vst[r][:, :]).then_inc(v_out[r], 16)

            def load_v(g, h):
                cols = slice(g * GDIM, (g + 1) * GDIM) if isinstance(g, int) else bass.ds(g * GDIM, GDIM)
                act.dma_start(v_raw[h][:, :, :], v_scratch[4 * h:4 * h + 4, :, cols].rearrange("t p n -> p t n")
                              ).then_inc(v_in[h], 16)

            def load_ws(g):
                if isinstance(g, int):
                    w_src, b_src = w_s_t[g], b_s[g:g + 1, :]
                else:
                    w_src = w_s_t[bass.ds(g, 1), :, :].rearrange("g q p -> (g q) p")
                    b_src = b_s[bass.ds(g, 1), :]
                act.dma_start(ws_raw[:, :], w_src).then_inc(ws_in, 16)
                act.dma_start(bs[:, :], b_src.broadcast_to([P, P])).then_inc(ws_in, 16)

            def hi_of_event(s, it, j, dst):
                act.wait_ge(s.full, it * 4 + (j + 1))
                h, f = divmod(j, 2)
                act.activation(dst[:, f, toks(h)], full[f][:, :], ACT.Copy).then_inc(s.hi, 1)

            def gmlp(it, first, last):
                s = hid["G"]
                act.wait_ge(ws_masked, it + 1)
                ge(act, s.mm, it * 4)
                act.activation(ws_hi[:, :], ws_raw[:, :], ACT.Copy).then_inc(ws_hi_done, 1)

                def event(j):
                    h, f = divmod(j, 2)
                    if f == 0:
                        act.wait_ge(v_in[h], (it + 1) * 16)
                        ge(act, s.mm, it * 4 + 2 * h)
                        for t in range(4):
                            act.activation(v_hi[:, t, :], v_raw[h][:, t, :], ACT.Copy,
                                           scale=rv[:, 4 * h + t:4 * h + t + 1]).then_inc(vs_hi, 1)
                    act.wait_ge(s.mm, it * 4 + (j + 1))
                    act.activation(atmp[f][:, :], bank[2 * f + 1][:, :], ACT.Gelu_apprx_tanh).then_inc(s.act, 1)
                    hi_of_event(s, it, j, y_hi)

                for j in range(3):
                    event(j)
                if last:
                    last_half(1, lambda: event(3))
                    return
                event(3)
                act.wait_ge(vs_lo, (it + 1) * 8)
                for h in range(NH2):
                    load_v(it + 1, h)
                act.wait_ge(ws_lo_done, it + 1)
                load_ws(it + 1)

            def ffn(name, n):
                def one(it, first, last):
                    s = hid[name]

                    def event(j):
                        f = j % 2
                        act.wait_ge(s.mm, it * 4 + (j + 1))
                        act.activation(atmp[f][:, :], bank[2 * f][:, :], ACT.Silu).then_inc(s.act, 1)
                        hi_of_event(s, it, j, h_hi)

                    for j in range(4):
                        if last and j == 3:
                            last_half(n, lambda: event(3))
                        else:
                            event(j)
                        if first and j == 0:
                            hi_tiles(n - 1, 1)
                return one

            def load_bias(pair):
                act.dma_start(bias[:, :, :], bass.AP(rel_scratch_t, pair * (2 * REV), [[1, P], [REV, 2], [1, WIN]])
                              ).then_inc(bias_in, 16)

            def p_hi_part(it, what, i, dst, src=None, scale=1.0):
                act.wait_ge(p_done, p_number(it, what, i) + 1)
                act.activation(dst, src if src is not None else p_bank(it, what, i)[:, :], ACT.Copy,
                               scale=scale).then_inc(p_hi, 1)

            def attention(it, first, last):
                def query_hi(it, h, name="q"):
                    p_hi_part(it, name, h, flipped(q_hi[:, toks(h)]), tiled(p_bank(it, name, h)[:, :]), HD ** -0.5)

                if first:
                    load_bias(0)
                    query_hi(-1, 0)
                    p_hi_part(it, "k", 0, k_hi[:, toks(0)])
                    hi_tiles(2, 1)
                    query_hi(0, 1, "q first")
                else:
                    p_hi_part(it, "k", 0, k_hi[:, toks(0)])
                p_hi_part(it, "k", 1, k_hi[:, toks(1)])
                for m in range(19):
                    if m == 2:
                        for h in range(NH2):
                            p_hi_part(it, "vt", h, in_heads(vz_hi, h), by_head(p_bank(it, "vt", h)))
                    if 0 <= m - 2 < 16:
                        s = m - 2
                        off = max(0, LEFT - s // 2) * P
                        act.wait_ge(t_done, it * 16 + (s + 1))
                        ge(act, pv_done, it * 16 + (s - 1))
                        act.activation(pt_hi[s % 2][:, off:], probs_t[:, off:WIN], ACT.Copy).then_inc(pt_hi_done, 1)
                    if m < 16:
                        off = max(0, LEFT - m // 2) * P
                        act.wait_ge(neg_done, it * 16 + (m + 1))
                        act.activation(prob[m % 2][:, off:], prob[m % 2][:, off:], ACT.Exp,
                                       bias=negmax[:, m % 2:m % 2 + 1],
                                       accum_out=rowsum[:, m % 2:m % 2 + 1]).then_inc(exp_done, 1)
                    if m == 15 and not last:
                        load_bias(it + 1)
                    if m in (10, 18):
                        act.wait_ge(pv_done, it * 16 + (8 if m == 10 else 16))
                        if m == 18 or not first:
                            act.wait_ge(p_done, p_number(it, "out0" if m == 18 else "out1p", 7) + 1)
                        act.activation(flipped(o_hi[:, :]), tiled(bank[3][:, :]), ACT.Copy).then_inc(o_hi_done, 1)
                    if m == 15 and not last:
                        query_hi(it, 0)
                    if m >= 12 and last:
                        square(3, 0, m - 12)
                if not last:
                    query_hi(it, 1)
                else:
                    squares(3, 0, 7)
                    std(3, 0)
                    hi_tiles(3, 0)
                    squares(3, 1)
                    std(3, 1)

            act.wait_ge(consts, 1)
            for h in range(NH2):
                squares(0, h)
                std(0, h)
                hi_tiles(0, h)
            act.wait_ge(hn_done, 16)
            repeat(act, CB, v_block)
            act.wait_ge(v_sum, CB)
            act.activation(rv[:, :], ssq[:, :], ACT.Sqrt, bias=eps[:, 0:1], scale=1.0 / GMLP).then_inc(rv_std, 1)
            for r in range(4):
                act.wait_ge(v_out[r], 2 * CB * 16)
            act.wait_ge(rel_out, 16)
            for h in range(NH2):
                load_v(0, h)
            load_ws(0)
            act.wait_ge(rv_done, 1)
            repeat(act, GROUPS, gmlp)
            repeat(act, CHUNKS, ffn("F1", 2))
            repeat(act, PAIRS, attention)
            repeat(act, CHUNKS, ffn("F2", 4))

        @block.vector
        def _(dve):
            def add_squares(n, h, k):
                base = 7 * (NH2 * n + h)
                dve.wait_ge(sq_done, 8 * (NH2 * n + h) + k + 1)
                ge(dve, acc_done, base + k - 1)
                dve.tensor_tensor(acc[:, :], acc[:, :], atmp[k % 2][:, :], ALU.add).then_inc(acc_done, 1)

            def inverse(n, h):
                dve.wait_ge(std_done, NH2 * n + h + 1)
                dve.reciprocal(rstd[h][:, :], rstd[h][:, :]).then_inc(rstd_done, 1)
                dve.wait_ge(rstd_done, NH2 * n + h + 1)

            def tile_full(n, h, k):
                e = 16 * n + 8 * h + k
                if n < 4 and (h or k >= 2):
                    dve.wait_ge(hn_done, e - 1)
                dst = full[k % 2][:, :] if n < 4 else x[:, k, toks(h)]
                dve.scalar_tensor_tensor(dst, x[:, k, toks(h)], gain[:, n, k:k + 1], rstd[h][:, :], ALU.mult,
                                         ALU.mult).then_inc(hn_full if n < 4 else y_full, 1)

            def tile_lo(n, h, k):
                if n < 4:
                    dve.wait_ge(hn_hi_done, 16 * n + 8 * h + k + 1)
                    dve.tensor_tensor(hn_lo[:, k, toks(h)], full[k % 2][:, :], r32(hn_hi[:, k, toks(h)]),
                                      ALU.subtract).then_inc(hn_done, 1)

            def tiles(n, h):
                for k in range(KT + 1):
                    if k < KT:
                        tile_full(n, h, k)
                    if k:
                        tile_lo(n, h, k - 1)

            def sum_squares(n, h, add=lambda k: None):
                for k in range(KT):
                    add(k)
                    if k:
                        add_squares(n, h, k)

            def tile_ops(n, h):
                ops = [lambda: tile_full(n, h, 0)]
                for k in range(1, KT):
                    ops.append(lambda k=k: tile_full(n, h, k))
                    if n < 4:
                        ops.append(lambda k=k: tile_lo(n, h, k - 1))
                return ops + ([lambda: tile_lo(n, h, KT - 1)] if n < 4 else [])

            def last_half(s, it, n, add, event_3):
                sum_squares(n, 0, lambda k: add(0, k))
                if n == 1:
                    event_3()
                inverse(n, 0)
                if n > 1:
                    event_3()
                dve.wait_ge(s.lo, it * 4 + 4)
                ops = tile_ops(n, 0)
                for k in range(KT):
                    ops[k]()
                    add(1, k)
                for op in ops[KT:]:
                    op()
                sum_squares(n, 1)
                inverse(n, 1)

            vst = [atmp[0], atmp[1], full[0], full[1]]

            def v_block(it, first, last):
                for t in range(BLOCKS):
                    dve.wait_ge(v_gelu, it * 8 + (t + 1))
                    ge(dve, v_ssq, it * 8 + t)
                    if t == 0:
                        ge(dve, v_sum, it * 1)
                    dve.tensor_tensor_reduce(mixed[:, :], vst[t % 4][:, :], vst[t % 4][:, :], 1.0, 0.0, ALU.mult,
                                             ALU.add, ssq_part[:, t:t + 1]).then_inc(v_ssq, 1)
                dve.wait_ge(v_ssq, it * 8 + 8)
                dve.tensor_tensor(ssq[:, :], ssq[:, :], ssq_part[:, :], ALU.add).then_inc(v_sum, 1)

            def split_product(s, it, j, lo, hi_part, in1, up):
                h, f = divmod(j, 2)
                ge(dve, s.lo, it * 4 + (j - 1))
                dve.tensor_tensor(full[f][:, :], up, in1, ALU.mult).then_inc(s.full, 1)
                dve.wait_ge(s.hi, it * 4 + (j + 1))
                dve.tensor_tensor(lo[:, f, toks(h)], full[f][:, :], r32(hi_part[:, f, toks(h)]),
                                  ALU.subtract).then_inc(s.lo, 1)

            def adds(s, it):
                def add(h, n):
                    d = 8 * h + n
                    dve.wait_ge(s.down, it * 16 + (d + 1))
                    dve.tensor_tensor(x[:, n, toks(h)], bank[4 + d % 4][:, :], x[:, n, toks(h)],
                                      ALU.add).then_inc(s.added, 1)
                return add

            def all_adds(s, it):
                add = adds(s, it)
                for h in range(NH2):
                    for k in range(KT):
                        add(h, k)

            def gmlp(it, first, last):
                s = hid["G"]
                dve.wait_ge(ws_in, (it + 1) * 32)
                dve.memset(ws_raw[CHUNK:P, 0:CHUNK], 0.0).then_inc(ws_masked, 1)
                dve.wait_ge(ws_hi_done, it + 1)
                dve.tensor_tensor(ws_lo[:, :], ws_raw[:, :], r32(ws_hi[:, :]), ALU.subtract).then_inc(ws_lo_done, 1)

                def event(j):
                    h, f = divmod(j, 2)
                    if f == 0:
                        for t in range(4):
                            dve.wait_ge(vs_hi, it * 8 + (4 * h + t + 1))
                            dve.scalar_tensor_tensor(v_lo[:, t, :], v_raw[h][:, t, :], rv[:, 4 * h + t:4 * h + t + 1],
                                                     r32(v_hi[:, t, :]), ALU.mult, ALU.subtract).then_inc(vs_lo, 1)
                    dve.wait_ge(s.mm, it * 4 + (j + 1))
                    ge(dve, s.full, it * 4 + j)
                    g_col = vgain[:, 2 * it + f:2 * it + f + 1] if isinstance(it, int) else vgain[:, bass.ds(it * 2 + f, 1)]
                    dve.scalar_tensor_tensor(tiled(mixed[:, :]), tiled(bank[2 * f][:, :]), g_col,
                                             bs[:, None, :].broadcast_to([P, 4, P]), ALU.mult, ALU.add).then_inc(mix_done, 1)
                    dve.wait_ge(mix_done, it * 4 + (j + 1))
                    dve.wait_ge(s.act, it * 4 + (j + 1))
                    split_product(s, it, j, y_lo, y_hi, atmp[f][:, :], mixed[:, :])

                for j in range(3):
                    event(j)
                if last:
                    last_half(s, it, 1, adds(s, it), lambda: event(3))
                else:
                    event(3)
                    all_adds(s, it)

            def ffn(name, n):
                def one(it, first, last):
                    s = hid[name]

                    def event(j):
                        f = j % 2
                        dve.wait_ge(s.act, it * 4 + (j + 1))
                        split_product(s, it, j, h_lo, h_hi, atmp[f][:, :], bank[2 * f + 1][:, :])

                    for j in range(3):
                        event(j)
                        if first and j == 0:
                            dve.wait_ge(s.lo, 1)
                            tiles(n - 1, 1)
                            dve.wait_ge(hn_done, 16 * n)
                    if last:
                        last_half(s, it, n, adds(s, it), lambda: event(3))
                        if n == 4:
                            tiles(4, 1)
                    else:
                        event(3)
                        all_adds(s, it)
                return one

            def p_lo_part(it, what, i, number, dst, hi_part, src=None):
                src = src if src is not None else p_bank(it, what, i)[:, :]
                dve.wait_ge(p_hi, it * 6 + (2 + number))
                dve.tensor_tensor(dst, src, hi_part, ALU.subtract).then_inc(p_read, 1)

            def query_lo(it, h, name="q", number=None):
                dve.wait_ge(p_hi, it * 6 + (2 + 5 + h) if number is None else number)
                dve.scalar_tensor_tensor(flipped(q_lo[:, toks(h)]), tiled(p_bank(it, name, h)[:, :]), HD ** -0.5,
                                         flipped(r32(q_hi[:, toks(h)])), ALU.mult, ALU.subtract).then_inc(p_read, 1)

            def mask_bias(it):
                dve.wait_ge(bias_in, (it + 1) * 16)
                dve.memset(bias[CHUNK:P, :, WIN - CHUNK:WIN], MASKED).then_inc(bias_masked, 1)
                dve.memset(bias[0:CHUNK, :, 0:CHUNK], MASKED).then_inc(bias_masked, 1)

            def attention(it, first, last):
                def out_add(name, h, n):
                    dve.wait_ge(p_done, p_number(it, name, n) + 1)
                    dve.tensor_tensor(x[:, n, toks(h)], p_bank(it, name, n)[:, :], x[:, n, toks(h)],
                                      ALU.add).then_inc(p_read, 1)

                def v_copy(h):
                    dve.wait_ge(p_done, p_number(it, "v", h) + 1)
                    dve.tensor_copy(atmp[h][:, :], p_bank(it, "v", h)[:, :]).then_inc(p_read, 1)

                def keys_lo(h, number):
                    p_lo_part(it, "k", h, number, k_lo[:, toks(h)], r32(k_hi[:, toks(h)]))

                if first:
                    query_lo(-1, 0, "q", 1)
                    keys_lo(0, 0)
                    v_copy(0)
                    tiles(2, 1)
                    query_lo(0, 1, "q first", 3)
                    keys_lo(1, 2)
                    for part in (vz_hi, vz_lo):
                        for head in range(2):
                            dve.memset(r32(part[:, :, head, (1 - head) * HD:(2 - head) * HD]), 0.0).then_inc(vz_zero, 1)
                    mask_bias(0)
                else:
                    for h in range(NH2):
                        keys_lo(h, 1 + h)
                for m in range(19):
                    if 0 <= m - 1 < 16:
                        s = m - 1
                        off = max(0, LEFT - s // 2) * P
                        c = slice(s % 2, s % 2 + 1)
                        dve.wait_ge(exp_done, it * 16 + (s + 1))
                        dve.reciprocal(rowinv[:, c], rowsum[:, c]).then_inc(inv_done, 1)
                        dve.wait_ge(inv_done, it * 16 + (s + 1))
                        dve.tensor_scalar(prob[s % 2][:, off:], prob[s % 2][:, off:], rowinv[:, c], None,
                                          ALU.mult).then_inc(normed, 1)
                    if m < 16:
                        off = max(0, LEFT - m // 2) * P
                        c = slice(m % 2, m % 2 + 1)
                        dve.wait_ge(qk_done, it * 16 + (m + 1))
                        if m == 0:
                            dve.wait_ge(bias_masked, it * 2 + 2)
                        ge(dve, t_done, it * 16 + (m - 1))
                        dve.sem_inc(step_begun)
                        dve.tensor_tensor_reduce(prob[m % 2][:, off:], scores[:, SHIFT + off:SHIFT + WIN],
                                                 bias[:, m % 2, off:], 1.0, -3.0e38, ALU.add, ALU.max,
                                                 rowmax[:, c]).then_inc(biased, 1)
                        dve.wait_ge(biased, it * 16 + (m + 1))
                        dve.tensor_scalar(negmax[:, c], rowmax[:, c], -1.0, None, ALU.mult).then_inc(neg_done, 1)
                    if m < 2 and not (first and m == 0):
                        v_copy(m)
                    if m == 2:
                        for h in range(NH2):
                            p_lo_part(it, "vt", h, 3 + h, in_heads(vz_lo, h), in_heads(vz_hi, h, r32),
                                      by_head(p_bank(it, "vt", h)))
                    if 0 <= m - 2 < 16:
                        s = m - 2
                        off = max(0, LEFT - s // 2) * P
                        dve.wait_ge(pt_hi_done, it * 16 + (s + 1))
                        dve.tensor_tensor(pt_lo[s % 2][:, off:], probs_t[:, off:WIN], r32(pt_hi[s % 2][:, off:]),
                                          ALU.subtract).then_inc(pt_lo_done, 1)
                    if m == 15 and not last:
                        query_lo(it, 0)
                    for n in OUT1P.get(m, ()) if not first else ():
                        out_add("out1p", 1, n)
                    if m in (10, 18):
                        dve.wait_ge(o_hi_done, it * 2 + (1 if m == 10 else 2))
                        dve.tensor_tensor(flipped(o_lo[:, :]), tiled(bank[3][:, :]), flipped(r32(o_hi[:, :])),
                                          ALU.subtract).then_inc(o_lo_done, 1)
                    if m >= 11:
                        out_add("out0", 0, m - 11)
                    if m >= 14 and last:
                        add_squares(3, 0, m - 13)
                if not last:
                    mask_bias(it + 1)
                    query_lo(it, 1)
                    return
                for k in (6, 7):
                    add_squares(3, 0, k)
                for k in range(2):
                    out_add("out1", 1, k)
                inverse(3, 0)
                for k in range(2, KT):
                    out_add("out1", 1, k)
                tiles(3, 0)
                sum_squares(3, 1)
                inverse(3, 1)

            dve.memset(ones[:, :], 1.0 / D)
            dve.memset(eps[:, :], EPS)
            dve.memset(ssq[:, :], 0.0)
            dve.drain().then_inc(consts, 1)
            dve.wait_ge(rel_in, 16)
            lead = WIN - P - 1
            dve.tensor_copy(rel_pad[:, 0:lead], rel[:, 0:1].broadcast_to([HEADS, lead])).then_inc(rel_padded, 1)
            dve.tensor_copy(rel_pad[:, lead:lead + N_REL], rel).then_inc(rel_padded, 1)
            dve.tensor_copy(rel_pad[:, lead + N_REL:], rel[:, N_REL - 1:N_REL].broadcast_to([HEADS, REV - lead - N_REL])
                            ).then_inc(rel_padded, 1)
            dve.wait_ge(small_in, 48)
            for h in range(NH2):
                sum_squares(0, h)
                inverse(0, h)
                tiles(0, h)
            repeat(dve, CB, v_block)
            dve.wait_ge(rv_std, 1)
            dve.reciprocal(rv[:, :], rv[:, :]).then_inc(rv_done, 1)
            dve.wait_ge(rv_done, 1)
            repeat(dve, GROUPS, gmlp)
            repeat(dve, CHUNKS, ffn("F1", 2))
            repeat(dve, PAIRS, attention)
            repeat(dve, CHUNKS, ffn("F2", 4))


def kernel(x, norm_mix_g, norm_ffn_g, final_g, a_w_in, a_v_gain, a_w_s, a_b_s, a_w_out, b_w_qkv, b_rel_bias,
           b_w_out, ffn_w_gate, ffn_w_up, ffn_w_down):
    import numpy as np
    import concourse.bacc as bacc
    from concourse.bass_utils import run_bass_kernel_spmd

    def tile_of(w, n):
        return w[:, n * P:(n + 1) * P].reshape(KT, P, P).transpose(1, 0, 2).reshape(P, UNIT)

    def rows_of(w, n):
        return w[n * P:(n + 1) * P, :]

    a = [np.asarray(t) for t in (a_w_in, a_w_out, b_w_qkv, b_w_out, ffn_w_gate, ffn_w_up, ffn_w_down)]
    w_in, w_out, w_qkv, w_o = (t[0] for t in a[:4])
    gate, up, down = a[4:]
    units = np.empty((UNITS, P, UNIT), np.float32)
    at = 0

    def put(unit):
        nonlocal at
        units[at] = unit
        at += 1

    for cb in range(CB):
        for j in range(4):
            v = w_in[2 * j * P:(2 * j + 2) * P, GMLP + cb * 512:GMLP + (cb + 1) * 512]
            put(v.reshape(2, P, 512).transpose(1, 0, 2).reshape(P, UNIT))
    for g in range(GROUPS):
        put(tile_of(w_in, 2 * g)), put(tile_of(w_in, 2 * g + 1))
        put(rows_of(w_out, 2 * g)), put(rows_of(w_out, 2 * g + 1))

    def ffn(i):
        for c in range(CHUNKS):
            for f in (2 * c, 2 * c + 1):
                put(tile_of(gate[i], f)), put(tile_of(up[i], f))
            put(rows_of(down[i], 2 * c)), put(rows_of(down[i], 2 * c + 1))

    ffn(0)
    put(tile_of(w_qkv, 0))
    for pair in range(PAIRS):
        put(tile_of(w_qkv, KT + pair)), put(tile_of(w_qkv, 2 * KT + pair))
        if pair < PAIRS - 1:
            put(tile_of(w_qkv, pair + 1))
        put(rows_of(w_o, pair))
    ffn(1)

    g = np.stack([np.asarray(t) for t in (norm_mix_g[0], norm_ffn_g[0], norm_mix_g[1], norm_ffn_g[1], final_g)])
    arrays = {
        "x_t": np.asarray(x)[0].T.reshape(KT, P, SEQ),
        "gains": g.reshape(5, KT, P).transpose(2, 0, 1),
        "v_gain": np.asarray(a_v_gain)[0].reshape(GMLP // P, P).T,
        "w_s_t": np.asarray(a_w_s)[0].transpose(0, 2, 1),
        "b_s": np.asarray(a_b_s)[0],
        "rel_rev": np.asarray(b_rel_bias)[0][:, ::-1],
        "ident": np.eye(P, dtype=np.float32),
        "w_units": units,
    }
    arrays = {name: np.ascontiguousarray(t) for name, t in arrays.items()}
    nc = bacc.Bacc("TRN2", target_bir_lowering=False, num_devices=1)
    ins = [nc.dram_tensor(name + "_in", t.shape, F32, kind="ExternalInput").ap() for name, t in arrays.items()]
    out = nc.dram_tensor("out_t", (KT, P, SEQ), F32, kind="ExternalOutput").ap()
    trunk(nc, *ins, out)
    r = run_bass_kernel_spmd(nc, [{name + "_in": t for name, t in arrays.items()}], core_ids=[0])
    return np.ascontiguousarray(r.results[0]["out_t"].reshape(D, SEQ).T).reshape(1, SEQ, D)
```

```python
from contextlib import ExitStack

import concourse.bass as bass
from concourse import mybir

F32 = mybir.dt.float32
F32R = mybir.dt.float32r
ALU = mybir.AluOpType
ACT = mybir.ActivationFunctionType

P = 128
SEQ = 1024
D = 1024
KT = D // P
HALF = SEQ // 2
NH2 = SEQ // HALF
UNIT = 1024
CHUNK = 64
EPS = 1e-6

GMLP = 2 * D
GROUPS = 8
GDIM = GMLP // GROUPS
BLOCKS = SEQ // P
CB = GMLP // 512

HEADS = 16
HD = D // HEADS
PAIRS = HEADS // 2
LEFT = 8 * CHUNK // P
WIN = (LEFT + 1) * P
N_REL = 192
SHIFT = P
SPLIT = 512 - SHIFT
REV = WIN + P - 1
MASKED = -1e30

D_FF = 2816
CHUNKS = D_FF // (2 * P)

Y_DVE = 5
RAW = 2
RING = 6

U_V = CB * 4
U_G = GROUPS * 4
U_F = CHUNKS * 6
U_B = PAIRS * 4
B_V, B_G = 0, U_V
B_F1 = B_G + U_G
B_B = B_F1 + U_F
B_F2 = B_B + U_B
UNITS = B_F2 + U_F


def ge(eng, sem, value):
    if isinstance(value, int) and value <= 0:
        return
    eng.wait_ge(sem, value)


def repeat(eng, n, body):
    body(0, True, False)
    with eng.Fori(1, n - 1) as it:
        body(it, False, False)
    body(n - 1, False, True)


def trunk(nc, x_t, gains, v_gain, w_s_t, b_s, rel_rev, ident_d, w_units, out_t):
    v_scratch = nc.dram_tensor("v_scratch", [BLOCKS, P, GMLP], F32).ap()
    rel_scratch_t = nc.dram_tensor("rel_scratch", [HEADS, REV], F32)
    rel_scratch = rel_scratch_t.ap()

    with ExitStack() as ctx:
        def sb(name, shape, dt=F32, at=ctx):
            return at.enter_context(nc.sbuf_tensor(name, shape, dt))

        def sem(name):
            return ctx.enter_context(nc.semaphore(name))

        bank = [ctx.enter_context(nc.psum_tensor(f"bank{i}", [P, 512], F32)) for i in range(4)]
        scores = ctx.enter_context(nc.psum_tensor("scores", [P, 1024], F32))
        probs_t = ctx.enter_context(nc.psum_tensor("probs_t", [P, 1024], F32))
        bank += [scores[:, 0:512], scores[:, 512:1024], probs_t[:, 0:512], probs_t[:, 512:1024]]

        x = sb("x", [P, KT, SEQ])
        hn_hi = sb("hn_hi", [P, KT, SEQ], F32R)
        hn_lo = sb("hn_lo", [P, KT, SEQ], F32R)
        raw = [sb(f"raw{i}", [P, UNIT]) for i in range(RAW)]
        w_hi = [sb(f"w_hi{i}", [P, UNIT], F32R) for i in range(4)]
        w_lo = [sb(f"w_lo{i}", [P, UNIT], F32R) for i in range(4)]
        atmp = [sb(f"atmp{i}", [P, HALF]) for i in range(2)]
        with ExitStack() as n:
            acc = sb("acc", [P, HALF], F32, n)
            full = [sb(f"full{i}", [P, HALF], F32, n) for i in range(2)]
            rstd = [sb(f"rstd{h}", [P, HALF], F32, n) for h in range(NH2)]
        pt_hi, pt_lo = ([sb(f"pt_{name}0", [P, 2 * WIN // P, P], F32R)] for name in ("hi", "lo"))
        ones = sb("ones", [P, P])
        ident = sb("ident", [P, P])
        gain = sb("gain", [P, 5, KT])
        vgain = sb("vgain", [P, GMLP // P])
        eps = sb("eps", [P, 1])
        ssq = sb("ssq", [P, BLOCKS])
        ssq_part = sb("ssq_part", [P, BLOCKS])
        rv = sb("rv", [P, BLOCKS])
        rowmax = sb("rowmax", [P, 2])
        negmax = sb("negmax", [P, 2])
        rowsum = sb("rowsum", [P, 2])
        rowinv = sb("rowinv", [P, 2])

        with ExitStack() as a:
            y_hi = sb("y_hi", [P, 2, SEQ], F32R, a)
            y_lo = sb("y_lo", [P, 2, SEQ], F32R, a)
            v_raw = [sb(f"v_raw{i}", [P, 4, GDIM], F32, a) for i in range(NH2)]
            v_hi = sb("v_hi", [P, 4, GDIM], F32R, a)
            v_lo = sb("v_lo", [P, 4, GDIM], F32R, a)
            mixed = sb("mixed", [P, HALF], F32, a)
            ws_raw = sb("ws_raw", [P, P], F32, a)
            ws_hi = sb("ws_hi", [P, P], F32R, a)
            ws_lo = sb("ws_lo", [P, P], F32R, a)
            bs = sb("bs", [P, P], F32, a)
        with ExitStack() as f:
            w_hi += [sb(f"w_hi{i}", [P, UNIT], F32R, f) for i in (4, 5)]
            w_lo += [sb(f"w_lo{i}", [P, UNIT], F32R, f) for i in (4, 5)]
            h_hi = sb("h_hi", [P, 2, SEQ], F32R, f)
            h_lo = sb("h_lo", [P, 2, SEQ], F32R, f)
        q_hi = sb("q_hi", [P, SEQ], F32R)
        q_lo = sb("q_lo", [P, SEQ], F32R)
        k_hi = sb("k_hi", [P, SEQ], F32R)
        k_lo = sb("k_lo", [P, SEQ], F32R)
        vz_hi = sb("vz_hi", [P, BLOCKS, 2, P], F32R)
        vz_lo = sb("vz_lo", [P, BLOCKS, 2, P], F32R)
        bias = sb("bias", [P, 2, WIN])
        prob = [sb(f"prob{i}", [P, WIN]) for i in range(2)]
        pt_hi += [sb("pt_hi1", [P, 2 * WIN // P, P], F32R)]
        pt_lo += [sb("pt_lo1", [P, 2 * WIN // P, P], F32R)]
        o_hi = sb("o_hi", [P, HALF], F32R)
        o_lo = sb("o_lo", [P, HALF], F32R)
        rel = v_raw[0][0:HEADS, :, :].rearrange("p t n -> p (t n)")[:, 0:N_REL]
        rel_pad = v_raw[1][0:HEADS, :, :].rearrange("p t n -> p (t n)")[:, 0:REV]

        taken, step_begun = sem("taken"), sem("step_begun")
        small_in = sem("small_in")
        rel_in, rel_padded, rel_out = sem("rel_in"), sem("rel_padded"), sem("rel_out")
        x_in = [[sem(f"x_in{h}_{k}") for k in range(KT)] for h in range(NH2)]
        consts = sem("consts")
        raw_in = [sem(f"raw_in{i}") for i in range(RAW)]
        w_split = sem("w_split")
        v_used = sem("v_used")
        sq_done, acc_done, mean_done = sem("sq_done"), sem("acc_done"), sem("mean_done")
        std_done, rstd_done = sem("std_done"), sem("rstd_done")
        hn_full, hn_hi_done, hn_done = sem("hn_full"), sem("hn_hi_done"), sem("hn_done")
        v_done, v_gelu, v_ssq, v_sum = sem("v_done"), sem("v_gelu"), sem("v_ssq"), sem("v_sum")
        v_out = [sem(f"v_out{i}") for i in range(4)]
        rv_std, rv_done = sem("rv_std"), sem("rv_done")
        v_in = [sem(f"v_in{i}") for i in range(NH2)]
        ws_in, ws_masked, ws_hi_done, ws_lo_done = sem("ws_in"), sem("ws_masked"), sem("ws_hi_done"), sem("ws_lo_done")
        vs_hi, vs_lo = sem("vs_hi"), sem("vs_lo")
        mix_done = sem("mix_done")

        class Hidden:
            def __init__(self, name):
                self.mm = sem(name + "_mm")
                self.act = sem(name + "_act")
                self.full = sem(name + "_full")
                self.hi = sem(name + "_hi")
                self.lo = sem(name + "_lo")
                self.down = sem(name + "_down")
                self.added = sem(name + "_added")

        hid = {"G": Hidden("g"), "F1": Hidden("f1"), "F2": Hidden("f2")}

        p_done, p_read = sem("p_done"), sem("p_read")
        p_hi = sem("p_hi")
        qk_done, biased, neg_done, exp_done = sem("qk_done"), sem("biased"), sem("neg_done"), sem("exp_done")
        inv_done, normed, t_done = sem("inv_done"), sem("normed"), sem("t_done")
        pt_hi_done, pt_lo_done, pv_done = sem("pt_hi_done"), sem("pt_lo_done"), sem("pv_done")
        o_hi_done, o_lo_done = sem("o_hi_done"), sem("o_lo_done")
        bias_in, bias_masked, vz_zero = sem("bias_in"), sem("bias_masked"), sem("vz_zero")
        y_full, y_pool = sem("y_full"), sem("y_pool")
        y_gained = sem("y_gained")
        y_out = sem("y_out")

        def r32(ap):
            return ap.bitcast(F32)

        def toks(h):
            return slice(h * HALF, (h + 1) * HALF)

        NORMS = ["load", "G", "F1", "B", "F2"]

        def x_final(eng, n, h, k):
            before = NORMS[n]
            if before == "load":
                eng.wait_ge(x_in[h][k], 16)
            elif before == "B":
                eng.wait_ge(p_read, p_number(PAIRS - 1, f"out{h}", k) + 1)
            else:
                its = GROUPS if before == "G" else CHUNKS
                eng.wait_ge(hid[before].added, 16 * (its - 1) + 8 * h + k + 1)

        def sums(n, h):
            return atmp[0] if (n, h) == (3, 0) else acc

        def square_buffer(n, h, k):
            return atmp[1 if (n, h) == (3, 0) else k % 2]

        def mean_bank(n, h):
            return bank[4 + h] if NORMS[n] in ("load", "B") else bank[4 * h]

        def out_events(name, lo, hi):
            return [((name, n), n % 2) for n in range(lo, hi)]

        order = {-1: [(("q", 0), 2)]}
        for pair in range(PAIRS):
            order[pair] = [(("k", 0), 0), (("k", 1), 1), (("v", 0), 2), (("vt", 0), 1), (("v", 1), 0), (("vt", 1), 2)]
            if pair == 0:
                order[pair][:3] = [(("k", 0), 0), (("v", 0), 1), (("q first", 1), 2), (("k", 1), 1)]
            if pair:
                order[pair] += out_events("out1p", 0, KT)
            if pair < PAIRS - 1:
                order[pair] += out_events("out0", 0, 3) + [(("q", 0), 2)] + out_events("out0", 3, KT) + [(("q", 1), 2)]
            else:
                order[pair] += out_events("out0", 0, KT) + [(("out1", n), 2 + n % 2) for n in range(KT)]
        plan = [(pair, event, b) for pair in order for event, b in order[pair]]
        number = {(pair, event): n for n, (pair, event, b) in enumerate(plan)}
        before = {(pair, event): max([m for m in range(n) if plan[m][2] == b], default=-1)
                  for n, (pair, event, b) in enumerate(plan)}
        bank_of = {(pair, event): bank[b] for pair, event, b in plan}
        P_BODY = len(order[1])

        def by_pair(table, it, event):
            if isinstance(it, int):
                return table[it, event]
            assert all(table[pair, event] == table[1, event] + (pair - 1) * P_BODY for pair in range(1, PAIRS - 1))
            return it * P_BODY + (table[1, event] - P_BODY)

        def p_number(it, what, i=0):
            return by_pair(number, it, (what, i))

        def p_bank(it, what, i=0):
            return bank_of[it if isinstance(it, int) else 1, (what, i)]

        V_1 = {0: (0, 1, 2), 1: (3, 4, 5, 6), 2: (7,)}
        OUT1P = {3: (0, 1), 4: (2,), 5: (3, 4), 6: (5,), 7: (6, 7)}
        OUT0 = {11: (0,), 12: (1,), 13: (2,), 14: (3,), 15: (4,), 16: (5,), 17: (6,), 18: (7,)}
        NEXT_Q = [{8: (0,), 9: (1, 2), 11: (3, 4), 13: (5, 6), 14: (7,)}, {16: (0, 1), 17: (2, 3), 18: (4, 5)}]

        def step(s):
            return 2 * (s // 4) + s % 2, s % 4 // 2

        def window(s):
            return max(0, LEFT - step(s)[0]) * P

        def pt_tiles(pt, s):
            return pt[s // 2 % 2][:, s % 2 * (WIN // P) + window(s) // P:(s % 2 + 1) * (WIN // P), :]

        def flipped(ap):
            return ap.rearrange("p (t c) -> p t c", c=P)[:, :, ::-1]

        def tiled(ap):
            return ap.rearrange("p (t c) -> p t c", c=P)

        def in_heads(vz, h, view=lambda ap: ap):
            return view(vz[:, 4 * h:4 * h + 4, :, :]).rearrange("p t a (b c) -> p t (a b) c", c=HD)[:, :, 0::3, :]

        def by_head(ap):
            return ap[:, :].rearrange("p (t a c) -> p t a c", t=4, a=2)

        block = ctx.enter_context(nc.Block())


        @block.sync
        def _(sp):
            def unit(u, r, split):
                ge(sp, w_split, split)
                src = w_units[u] if isinstance(u, int) else w_units[bass.ds(u, 1), :, :].rearrange("u p n -> (u p) n")
                sp.dma_start(raw[r][:, :], src).then_inc(raw_in[r], 16)

            def load_x(h):
                for k in range(KT):
                    sp.dma_start(x[:, k, toks(h)], x_t[k][:, toks(h)]).then_inc(x_in[h][k], 16)

            load_x(0)
            sp.dma_start(gain[:, :, :], gains).then_inc(small_in, 16)
            sp.dma_start(vgain[:, :], v_gain).then_inc(small_in, 16)
            sp.dma_start(ident[:, :], ident_d).then_inc(small_in, 16)
            sp.dma_start(rel, rel_rev).then_inc(rel_in, 16)
            for r in range(RAW):
                unit(r, r, 0)
            load_x(1)
            sp.wait_ge(rel_padded, 3)
            sp.dma_start(rel_scratch, rel_pad).then_inc(rel_out, 16)
            with sp.Fori(1, UNITS // RAW) as j:
                for r in range(RAW):
                    unit(j * RAW + r, r, j * (2 * RAW) + (2 * r - 2 * RAW + 2))
            for k in range(KT):
                sp.wait_ge(y_pool, k + 1)
                sp.dma_start(out_t[k][:, toks(0)], x[:, k, toks(0)]).then_inc(y_out, 16)
            for k in [0, 1, 5, 2, 3, 6, 4, 7]:
                if k < Y_DVE:
                    sp.wait_ge(y_full, k + 1)
                else:
                    sp.wait_ge(y_pool, KT + k - Y_DVE + 1)
                sp.dma_start(out_t[k][:, toks(1)], x[:, k, toks(1)]).then_inc(y_out, 16)
            sp.wait_ge(y_out, 16 * NH2 * KT)

        @block.gpsimd
        def _(pool):
            def split(u, r, loads, slot):
                pool.wait_ge(raw_in[r], loads)
                pool.sem_inc(taken)
                pool.tensor_scalar(w_hi[slot][:, :], raw[r][:, :], 1.0, 1.0, ALU.mult, ALU.mult).then_inc(w_split, 1)
                pool.wait_ge(w_split, u * 2 + 1)
                pool.tensor_tensor(w_lo[slot][:, :], raw[r][:, :], r32(w_hi[slot][:, :]),
                                   ALU.subtract).then_inc(w_split, 1)

            def units(base, count, per, used, peeled=1):
                def one(it):
                    for s in range(per):
                        used(it, s)
                        split(it * per + (base + s), (base + s) % RAW,
                              it * (16 * per // RAW) + 16 * ((base + s) // RAW + 1), s)
                for it in range(peeled):
                    one(it)
                with pool.Fori(peeled, count) as it:
                    one(it)

            def used_v(it, s):
                if s < 3:
                    ge(pool, v_used, it * 3 + (s - 2))
                else:
                    ge(pool, v_done, it * 8)

            def used_g(it, s):
                if isinstance(it, int):
                    pool.wait_ge(v_done, CB * BLOCKS)
                elif s < 2:
                    pool.wait_ge(hid["G"].mm, it * 4 + (s - 1))
                else:
                    pool.wait_ge(hid["G"].down, it * 16)

            def used_f(name):
                def used(it, s):
                    if not isinstance(it, int):
                        if s < 4:
                            pool.wait_ge(hid[name].mm, it * 4 + (s // 2 - 1))
                        else:
                            pool.wait_ge(hid[name].down, it * 16)
                    elif name == "F1":
                        if s < 2:
                            pool.wait_ge(hid["G"].mm, 4 * GROUPS - 1 + s)
                        else:
                            pool.wait_ge(hid["G"].down, 16 * GROUPS)
                    else:
                        pool.wait_ge(p_done, p_number(PAIRS - 1, *[("out1p", 7), ("k", 1), ("v", 1), ("out1", 7)][min(s, 3)]) + 1)
                return used

            def used_b(it, s):
                if isinstance(it, int) and it == 0:
                    pool.wait_ge(hid["F1"].mm, 4 * CHUNKS - 1 + s // 2)
                elif isinstance(it, int):
                    last = [number[0, ("q first", 1)], number[0, ("k", 1)], number[0, ("v", 1)], number[0, ("q", 1)]][s]
                    pool.wait_ge(p_done, last + 1)
                else:
                    last = p_number(1, *[("out1p", 7), ("k", 1), ("v", 1), ("q", 1)][s])
                    pool.wait_ge(p_done, it * P_BODY + (last + 1 - 2 * P_BODY))

            units(B_V, CB, 4, used_v)
            units(B_G, GROUPS, 4, used_g)
            units(B_F1, CHUNKS, 6, used_f("F1"))
            units(B_B, PAIRS, 4, used_b, peeled=2)
            units(B_F2, CHUNKS, 6, used_f("F2"))
            scaled = 0
            for h, tiles in ((0, range(KT)), (1, range(Y_DVE, KT))):
                pool.wait_ge(sq_done, 8 * (NH2 * 4 + h) + 8)
                for k in tiles:
                    pool.tensor_scalar(x[:, k, toks(h)], x[:, k, toks(h)], gain[:, 4, k:k + 1], None, ALU.mult
                                       ).then_inc(y_gained, 1)
                pool.wait_ge(rstd_done, 2 * (NH2 * 4 + h) + 2)
                for k in tiles:
                    scaled += 1
                    pool.wait_ge(y_gained, scaled)
                    pool.tensor_tensor(x[:, k, toks(h)], x[:, k, toks(h)], rstd[h][:, :], ALU.mult).then_inc(y_pool, 1)

        @block.tensor
        def _(pe):
            def product(out, lhs, rhs, start, stop, signal=None):
                (lh, ll), (rh, rl) = lhs, rhs
                pe.matmul(out, lh, rh, start=start, stop=False)
                pe.matmul(out, lh, rl, start=False, stop=False)
                last = pe.matmul(out, ll, rh, start=False, stop=stop)
                if signal is not None:
                    last.then_inc(signal, 1)

            def w(slot, lo, hi):
                return w_hi[slot][:, lo:hi], w_lo[slot][:, lo:hi]

            def hn(k, sl):
                return hn_hi[:, k, sl], hn_lo[:, k, sl]

            def project(outs, slot, unit, h, norm, signal=None, hooks=(), each=False):
                pe.wait_ge(w_split, (unit + (len(outs) - 1)) * 2 + 2)
                for k in range(KT):
                    pe.wait_ge(hn_done, 16 * norm + 8 * h + k + 1)
                    for i, out in enumerate(outs):
                        product(out, w(slot + i, k * P, (k + 1) * P), hn(k, toks(h)), k == 0, k == KT - 1,
                                signal if k == KT - 1 and (each or i == len(outs) - 1) else None)
                    for at, hook in hooks:
                        if at == k:
                            hook()

            def mean(n, h):
                pe.wait_ge(acc_done, 7 * (NH2 * n + h) + 7)
                pe.matmul(mean_bank(n, h)[:, :], ones[:, :], sums(n, h)[:, :], start=True, stop=True).then_inc(mean_done, 1)

            def v_block(it, first, last):
                for th in range(NH2):
                    for j in range(4):
                        if first and th == 0 and j == 3:
                            mean(0, 1)
                        pe.wait_ge(w_split, it * 8 + (2 * j + 2))
                        for kk in range(2):
                            k = 2 * j + kk
                            pe.wait_ge(hn_done, 8 * th + k + 1)
                            for t in range(4 * th, 4 * th + 4):
                                if k == 0:
                                    ge(pe, v_gelu, it * 8 + (t - 7))
                                end = t == 4 * th + 3 and kk == 1 and th == 1 and j < 3
                                product(bank[t][:, :], hn(k, slice(t * P, (t + 1) * P)), w(j, kk * 512, kk * 512 + 512),
                                        k == 0, k == KT - 1, v_done if k == KT - 1 else v_used if end else None)

            def hidden(name, u0, per, it, last, norm, event, hi, lo, hooks):
                s = hid[name]

                def make(j):
                    h, f = divmod(j, 2)
                    ge(pe, s.full, it * 4 + (j - 1))
                    event(it, h, f, s, hooks.get(j, ()))

                def share(h, n, f):
                    d = 8 * h + n
                    slot = per - 2 + f
                    if f == 0:
                        ge(pe, s.added, it * 16 + (d - 3))
                    product(bank[4 + d % 4][:, :], w(slot, n * P, (n + 1) * P),
                            (hi[:, f, toks(h)], lo[:, f, toks(h)]), f == 0, f == 1, s.down if f == 1 else None)

                def down(h, ahead=0):
                    if name == "G":
                        pe.wait_ge(v_gelu, CB * BLOCKS)
                    if h == 0:
                        pe.wait_ge(w_split, (it * per + (u0 + per - 1)) * 2 + 2)
                    if ahead:
                        pe.wait_ge(s.lo, it * 4 + (2 * h + 1))
                    for n in range(ahead):
                        share(h, n, 0)
                    pe.wait_ge(s.lo, it * 4 + (2 * h + 2))
                    for n in range(KT):
                        for f in range(2 if n >= ahead else 0):
                            share(h, n, f)
                        if n < ahead:
                            share(h, n, 1)

                if not last:
                    for j in range(4):
                        make(j)
                    down(0)
                    down(1)
                else:
                    for j in range(3):
                        make(j)
                    down(0)

                    def mean_0():
                        pe.wait_ge(s.full, it * 4 + 3)
                        mean(norm + 1, 0)
                    hooks = {3: ((KT - 1 if name == "G" else 2, mean_0),)}
                    make(3)
                    down(1, ahead=4)

            def gmlp_event(it, h, f, s, hooks):
                def u(f):
                    pe.wait_ge(v_gelu, (CB - 1) * BLOCKS + 2 * f + 2)
                    project([bank[2 * f + 1][:, :]], f, it * 4 + (B_G + f), h, 0, None, hooks)

                start = isinstance(it, int) and it == 0 and h == 0
                if not start:
                    u(f)
                elif f == 0:
                    u(0)
                    u(1)
                pe.wait_ge(vs_lo, it * 8 + (4 * h + 4))
                pe.wait_ge(ws_lo_done, it + 1)
                ch = slice(f * P, (f + 1) * P)
                for t in range(4):
                    product(bank[2 * f][:, t * P:(t + 1) * P], (v_hi[:, t, ch], v_lo[:, t, ch]),
                            (ws_hi[:, :], ws_lo[:, :]), True, True, s.mm if t == 3 else None)

            def ffn_event(u0, norm):
                def event(it, h, f, s, hooks):
                    project([bank[2 * f][:, :], bank[2 * f + 1][:, :]], 2 * f, it * 6 + (u0 + 2 * f), h, norm, s.mm, hooks)
                return event

            def fill(it, what, i=0):
                ge(pe, p_read, by_pair(before, it, (what, i)) + 1)
                return p_bank(it, what, i)

            def part(it, what, h, k, unit, slot):
                if k == 0:
                    fill(it, what, h)
                    pe.wait_ge(w_split, unit * 2 + 2)
                product(p_bank(it, what, h)[:, :], w(slot, k * P, (k + 1) * P), hn(k, toks(h)), k == 0, k == KT - 1,
                        p_done if k == KT - 1 else None)

            def out_product(it, name, n, slot):
                out = fill(it, name, n)
                if name == "out1p":
                    pe.wait_ge(o_lo_done, it * 2)
                product(out[:, :], w(slot, n * P, (n + 1) * P), (o_hi[:, :], o_lo[:, :]), True, True, p_done)

            def scores_of(it, s):
                i, head = step(s)
                rows = slice(head * HD, (head + 1) * HD)
                if s == 0:
                    pe.wait_ge(p_read, p_number(it, "k", 1) + 1)
                ge(pe, biased, it * 16 + s)
                off = window(s)
                tq = slice(i * P, (i + 1) * P)
                parts = ([(off, SPLIT)] if off < SPLIT else []) + [(max(off, SPLIT), WIN)]
                for at, to in parts:
                    tk = slice((i - LEFT) * P + at, (i - LEFT) * P + to)
                    product(scores[:, SHIFT + at:SHIFT + to], (q_hi[rows, tq], q_lo[rows, tq]), (k_hi[rows, tk], k_lo[rows, tk]),
                            True, True, qk_done if to == WIN else None)

            def transpose_probs(it, s):
                i = step(s)[0]
                pe.wait_ge(normed, it * 16 + (s + 1))
                ge(pe, pt_lo_done, it * 16 + s)
                for j in range(max(0, LEFT - i), LEFT + 1):
                    t = pe.transpose(probs_t[:, j * P:(j + 1) * P], prob[s % 2][:, j * P:(j + 1) * P], ident[:, :])
                t.then_inc(t_done, 1)

            def values(it, c):
                i, head = step(2 * c)
                pe.wait_ge(p_read, p_number(it, "vt", (i + 1) // 4) + 1)
                pe.wait_ge(pt_lo_done, it * 16 + (2 * c + 2))
                if c % 4 == 0:
                    ge(pe, o_lo_done, it * 2 + i // 4)
                both = [(key, 0, 2) for key in range(max(0, i - LEFT + 1), i + 1)]
                for key, q, n in both + ([(i - LEFT, 0, 1)] if i >= LEFT else []) + [(i + 1, 1, 1)]:
                    tiles = WIN // P
                    at = q * tiles + key - (i + q - LEFT)
                    cols = slice((i % 4 + q) * P, (i % 4 + q + n) * P)
                    out = bank[3][:, cols]
                    if n == 2:
                        out = tiled(out)
                    parts = [pt[c % 2][:, at:at + tiles:tiles - 1, :] if n == 2 else pt[c % 2][:, at, :]
                             for pt in (pt_hi, pt_lo)]
                    product(out, (vz_hi[:, key, head, :], vz_lo[:, key, head, :]), parts,
                            head == 0 and key == both[0][0] and n == 2, head == 1 and q == 1,
                            pv_done if q == 1 else None)

            def attention(it, first, last):
                u = it * 4 + B_B
                if first:
                    project([fill(-1, "q", 0)[:, :], fill(0, "k", 0)[:, :], fill(0, "v", 0)[:, :]], 0, u, 0, 2,
                            p_done, ((6, lambda: mean(2, 1)),), each=True)
                    project([fill(0, "q first", 1)[:, :], fill(0, "k", 1)[:, :]], 0, u, 1, 2, p_done, each=True)
                else:
                    for what, slot in (("k", 1), ("v", 2)):
                        for h in range(NH2 if what == "k" else 1):
                            for k in range(KT):
                                part(it, what, h, k, u + slot, slot)
                for m in range(19):
                    if 0 <= m - 2 < 16:
                        transpose_probs(it, m - 2)
                    if m < 16:
                        scores_of(it, m)
                    for k in V_1.get(m, ()):
                        part(it, "v", 1, k, u + 2, 2)
                    if m in (1, 3):
                        h = m // 2
                        pe.wait_ge(p_read, p_number(it, "v", h) + 1)
                        out = fill(it, "vt", h)
                        for t in range(4):
                            tr = pe.transpose(out[:, t * P:(t + 1) * P], atmp[h][:, t * P:(t + 1) * P], ident[:, :])
                        tr.then_inc(p_done, 1)
                    for h in range(NH2 if not last else 0):
                        for k in NEXT_Q[h].get(m, ()):
                            part(it, "q", h, k, u + 3, 3)
                    if m >= 4 and m % 2 == 0:
                        values(it, m // 2 - 2)
                    for n in OUT1P.get(m, ()) if not first else ():
                        out_product(it, "out1p", n, 0)
                    for n in OUT0.get(m, ()):
                        if n == 0:
                            pe.wait_ge(w_split, (u + (3 if last else 4)) * 2 + 2)
                            pe.wait_ge(o_lo_done, it * 2 + 1)
                        out_product(it, "out0", n, 3 if last else 0)
                if not last:
                    for k in range(1 + NEXT_Q[1][18][-1], KT):
                        part(it, "q", 1, k, u + 3, 3)
                    return
                pe.wait_ge(o_lo_done, it * 2 + 2)
                for n in range(KT):
                    out_product(it, "out1", n, 3)
                    if n == 1:
                        mean(3, 0)

            pe.wait_ge(small_in, 48)
            pe.wait_ge(consts, 1)
            mean(0, 0)
            repeat(pe, CB, v_block)
            def gmlp(it, first, last):
                hidden("G", B_G, 4, it, last, 0, gmlp_event, y_hi, y_lo, {})
            repeat(pe, GROUPS, gmlp)
            def ffn1(it, first, last):
                hooks = {1: ((1, lambda: mean(1, 1)),)} if first else {}
                hidden("F1", B_F1, 6, it, last, 1, ffn_event(B_F1, 1), h_hi, h_lo, hooks)
            repeat(pe, CHUNKS, ffn1)
            repeat(pe, PAIRS, attention)
            pe.wait_ge(p_read, p_number(PAIRS - 1, "out0", 7) + 1)
            def ffn2(it, first, last):
                def hook():
                    mean(3, 1)
                def banks_free():
                    pe.wait_ge(p_read, p_number(PAIRS - 1, "out1", 7) + 1)
                hooks = {0: ((KT - 1, banks_free),), 1: ((2, hook),)} if first else {}
                hidden("F2", B_F2, 6, it, last, 3, ffn_event(B_F2, 3), h_hi, h_lo, hooks)
            repeat(pe, CHUNKS, ffn2)
            mean(4, 1)

        @block.scalar
        def _(act):
            def square(n, h, k):
                x_final(act, n, h, k)
                halves = NH2 * n + h
                if k == 0:
                    ge(act, mean_done, halves)
                    dst = sums(n, h)
                else:
                    ge(act, acc_done, 7 * halves + max(0, k - (1 if (n, h) == (3, 0) else 2)))
                    dst = square_buffer(n, h, k)
                act.activation(dst[:, :], x[:, k, toks(h)], ACT.Square).then_inc(sq_done, 1)

            def std(n, h):
                act.wait_ge(mean_done, NH2 * n + h + 1)
                act.activation(rstd[h][:, :], mean_bank(n, h)[:, :], ACT.Sqrt, bias=eps[:, 0:1]).then_inc(std_done, 1)

            def squares(n, h, lo=0):
                for k in range(lo, KT):
                    square(n, h, k)

            def hi_tiles(n, h, lo=0, hi=KT):
                for k in range(lo, hi if n < 4 else 0):
                    act.wait_ge(hn_full, 16 * n + 8 * h + k + 1)
                    act.activation(hn_hi[:, k, toks(h)], full[k % 2][:, :], ACT.Copy).then_inc(hn_hi_done, 1)

            def last_half(n, event_3):
                squares(n, 0)
                if n == 1:
                    event_3()
                std(n, 0)
                if n > 1:
                    event_3()
                hi_tiles(n, 0)
                squares(n, 1)
                std(n, 1)

            vst = [atmp[0], atmp[1], full[0], full[1]]

            def v_block(it, first, last):
                for t in range(BLOCKS):
                    r = t % 4
                    act.wait_ge(v_done, it * 8 + (t + 1))
                    ge(act, v_ssq, it * 8 + (t - 3))
                    if not (first and t < 4):
                        act.wait_ge(v_out[r], it * 32 + 16 * (t // 4))
                    act.activation(vst[r][:, :], bank[t][:, :], ACT.Gelu_apprx_tanh).then_inc(v_gelu, 1)
                    act.wait_ge(v_gelu, it * 8 + (t + 1))
                    dst = v_scratch[t][:, it * 512:(it + 1) * 512] if isinstance(it, int) \
                        else v_scratch[t][:, bass.ds(it * 512, 512)]
                    act.dma_start(dst, vst[r][:, :]).then_inc(v_out[r], 16)

            def load_v(g, h):
                cols = slice(g * GDIM, (g + 1) * GDIM) if isinstance(g, int) else bass.ds(g * GDIM, GDIM)
                act.dma_start(v_raw[h][:, :, :], v_scratch[4 * h:4 * h + 4, :, cols].rearrange("t p n -> p t n")
                              ).then_inc(v_in[h], 16)

            def load_ws(g):
                if isinstance(g, int):
                    w_src, b_src = w_s_t[g], b_s[g:g + 1, :]
                else:
                    w_src = w_s_t[bass.ds(g, 1), :, :].rearrange("g q p -> (g q) p")
                    b_src = b_s[bass.ds(g, 1), :]
                act.dma_start(ws_raw[:, :], w_src).then_inc(ws_in, 16)
                act.dma_start(bs[:, :], b_src.broadcast_to([P, P])).then_inc(ws_in, 16)

            def hi_of_event(s, it, j, dst):
                act.wait_ge(s.full, it * 4 + (j + 1))
                h, f = divmod(j, 2)
                act.activation(dst[:, f, toks(h)], full[f][:, :], ACT.Copy).then_inc(s.hi, 1)

            def gmlp(it, first, last):
                s = hid["G"]
                act.wait_ge(ws_masked, it + 1)
                ge(act, s.mm, it * 4)
                act.activation(ws_hi[:, :], ws_raw[:, :], ACT.Copy).then_inc(ws_hi_done, 1)

                def event(j):
                    h, f = divmod(j, 2)
                    if f == 0:
                        act.wait_ge(v_in[h], (it + 1) * 16)
                        ge(act, s.mm, it * 4 + 2 * h)
                        for t in range(4):
                            act.activation(v_hi[:, t, :], v_raw[h][:, t, :], ACT.Copy,
                                           scale=rv[:, 4 * h + t:4 * h + t + 1]).then_inc(vs_hi, 1)
                    act.wait_ge(s.mm, it * 4 + (j + 1))
                    act.activation(atmp[f][:, :], bank[2 * f + 1][:, :], ACT.Gelu_apprx_tanh).then_inc(s.act, 1)
                    hi_of_event(s, it, j, y_hi)

                for j in range(3):
                    event(j)
                if last:
                    last_half(1, lambda: event(3))
                    return
                event(3)
                act.wait_ge(vs_lo, (it + 1) * 8)
                for h in range(NH2):
                    load_v(it + 1, h)
                act.wait_ge(ws_lo_done, it + 1)
                load_ws(it + 1)

            def ffn(name, n):
                def one(it, first, last):
                    s = hid[name]

                    def event(j):
                        f = j % 2
                        act.wait_ge(s.mm, it * 4 + (j + 1))
                        act.activation(atmp[f][:, :], bank[2 * f][:, :], ACT.Silu).then_inc(s.act, 1)
                        hi_of_event(s, it, j, h_hi)

                    for j in range(4):
                        if last and j == 3:
                            last_half(n, lambda: event(3))
                        else:
                            event(j)
                        if first and j == 0:
                            hi_tiles(n - 1, 1)
                return one

            def load_bias(pair):
                act.dma_start(bias[:, :, :], bass.AP(rel_scratch_t, pair * (2 * REV), [[1, P], [REV, 2], [1, WIN]])
                              ).then_inc(bias_in, 16)

            def p_hi_part(it, what, i, dst, src=None, scale=1.0):
                act.wait_ge(p_done, p_number(it, what, i) + 1)
                act.activation(dst, src if src is not None else p_bank(it, what, i)[:, :], ACT.Copy,
                               scale=scale).then_inc(p_hi, 1)

            def attention(it, first, last):
                def query_hi(it, h, name="q"):
                    p_hi_part(it, name, h, flipped(q_hi[:, toks(h)]), tiled(p_bank(it, name, h)[:, :]), HD ** -0.5)

                if first:
                    load_bias(0)
                    query_hi(-1, 0)
                    p_hi_part(it, "k", 0, k_hi[:, toks(0)])
                    hi_tiles(2, 1)
                    query_hi(0, 1, "q first")
                else:
                    p_hi_part(it, "k", 0, k_hi[:, toks(0)])
                p_hi_part(it, "k", 1, k_hi[:, toks(1)])
                for m in range(19):
                    if 0 <= m - 2 < 16:
                        s = m - 2
                        act.wait_ge(t_done, it * 16 + (s + 1))
                        ge(act, pv_done, it * 8 + (s // 2 - 1))
                        act.activation(pt_tiles(pt_hi, s), tiled(probs_t[:, window(s):WIN]), ACT.Copy
                                       ).then_inc(pt_hi_done, 1)
                    if 0 <= m - 1 < 16:
                        s = m - 1
                        act.wait_ge(inv_done, it * 16 + (s + 1))
                        act.activation(prob[s % 2][:, window(s):], prob[s % 2][:, window(s):], ACT.Copy,
                                       scale=rowinv[:, s % 2:s % 2 + 1]).then_inc(normed, 1)
                    if m < 16:
                        off = window(m)
                        act.wait_ge(neg_done, it * 16 + (m + 1))
                        act.activation(prob[m % 2][:, off:], prob[m % 2][:, off:], ACT.Exp,
                                       bias=negmax[:, m % 2:m % 2 + 1],
                                       accum_out=rowsum[:, m % 2:m % 2 + 1]).then_inc(exp_done, 1)
                    if m in (1, 3):
                        p_hi_part(it, "vt", m // 2, in_heads(vz_hi, m // 2), by_head(p_bank(it, "vt", m // 2)))
                    if m == 15 and not last:
                        load_bias(it + 1)
                    if m in (10, 18):
                        act.wait_ge(pv_done, it * 8 + (4 if m == 10 else 8))
                        if m == 18 or not first:
                            act.wait_ge(p_done, p_number(it, "out0" if m == 18 else "out1p", 7) + 1)
                        act.activation(flipped(o_hi[:, :]), tiled(bank[3][:, :]), ACT.Copy).then_inc(o_hi_done, 1)
                    if m == 14 and not last:
                        query_hi(it, 0)
                    if m >= 12 and last:
                        square(3, 0, m - 12)
                if not last:
                    query_hi(it, 1)
                else:
                    squares(3, 0, 7)
                    std(3, 0)
                    hi_tiles(3, 0)
                    squares(3, 1)
                    std(3, 1)

            act.wait_ge(consts, 1)
            for h in range(NH2):
                squares(0, h)
                std(0, h)
                hi_tiles(0, h)
            act.wait_ge(hn_done, 16)
            repeat(act, CB, v_block)
            act.wait_ge(v_sum, CB)
            act.activation(rv[:, :], ssq[:, :], ACT.Sqrt, bias=eps[:, 0:1], scale=1.0 / GMLP).then_inc(rv_std, 1)
            for r in range(4):
                act.wait_ge(v_out[r], 2 * CB * 16)
            act.wait_ge(rel_out, 16)
            for h in range(NH2):
                load_v(0, h)
            load_ws(0)
            act.wait_ge(rv_done, 1)
            repeat(act, GROUPS, gmlp)
            repeat(act, CHUNKS, ffn("F1", 2))
            repeat(act, PAIRS, attention)
            repeat(act, CHUNKS, ffn("F2", 4))

        @block.vector
        def _(dve):
            def add_squares(n, h, k):
                base = 7 * (NH2 * n + h)
                dve.wait_ge(sq_done, 8 * (NH2 * n + h) + k + 1)
                ge(dve, acc_done, base + k - 1)
                dve.tensor_tensor(sums(n, h)[:, :], sums(n, h)[:, :], square_buffer(n, h, k)[:, :],
                                  ALU.add).then_inc(acc_done, 1)

            def inverse(n, h, between=lambda: None):
                dve.wait_ge(std_done, NH2 * n + h + 1)
                for piece in range(2):
                    cols = slice(piece * HALF // 2, (piece + 1) * HALF // 2)
                    dve.reciprocal(rstd[h][:, cols], rstd[h][:, cols]).then_inc(rstd_done, 1)
                    if piece == 0:
                        between()
                dve.wait_ge(rstd_done, 2 * (NH2 * n + h) + 2)

            def tile_full(n, h, k):
                e = 16 * n + 8 * h + k
                if h or k >= 2:
                    dve.wait_ge(hn_done, e - 1)
                dve.scalar_tensor_tensor(full[k % 2][:, :], x[:, k, toks(h)], gain[:, n, k:k + 1], rstd[h][:, :],
                                         ALU.mult, ALU.mult).then_inc(hn_full, 1)

            def tile_lo(n, h, k):
                dve.wait_ge(hn_hi_done, 16 * n + 8 * h + k + 1)
                dve.tensor_tensor(hn_lo[:, k, toks(h)], full[k % 2][:, :], r32(hn_hi[:, k, toks(h)]),
                                  ALU.subtract).then_inc(hn_done, 1)

            def tiles(n, h):
                for k in range(KT + 1):
                    if k < KT:
                        tile_full(n, h, k)
                    if k:
                        tile_lo(n, h, k - 1)

            def sum_squares(n, h, add=lambda k: None):
                for k in range(KT + 1):
                    if k < KT:
                        add(k)
                    if k > 1:
                        add_squares(n, h, k - 1)

            def tile_ops(n, h):
                ops = [lambda: tile_full(n, h, 0)]
                for k in range(1, KT):
                    ops.append(lambda k=k: tile_full(n, h, k))
                    ops.append(lambda k=k: tile_lo(n, h, k - 1))
                return ops + [lambda: tile_lo(n, h, KT - 1)]

            def last_half(s, it, n, add, event_3):
                sum_squares(n, 0, lambda k: add(0, k))
                if n == 1:
                    event_3()
                    inverse(n, 0, lambda: add(1, 0))
                    add(1, 1)
                else:
                    inverse(n, 0)
                    event_3()
                if n == 4:
                    sum_squares(4, 1, lambda k: add(1, k))
                    inverse(4, 1)
                    return
                dve.wait_ge(s.lo, it * 4 + 4)
                ops = tile_ops(n, 0)
                for k in range(KT):
                    ops[k]()
                    if n > 1 or k > 1:
                        add(1, k)
                for op in ops[KT:]:
                    op()
                sum_squares(n, 1)
                inverse(n, 1)

            vst = [atmp[0], atmp[1], full[0], full[1]]

            def v_block(it, first, last):
                for t in range(BLOCKS):
                    dve.wait_ge(v_gelu, it * 8 + (t + 1))
                    ge(dve, v_ssq, it * 8 + t)
                    if t == 0:
                        ge(dve, v_sum, it * 1)
                    dve.tensor_tensor_reduce(mixed[:, :], vst[t % 4][:, :], vst[t % 4][:, :], 1.0, 0.0, ALU.mult,
                                             ALU.add, ssq_part[:, t:t + 1]).then_inc(v_ssq, 1)
                dve.wait_ge(v_ssq, it * 8 + 8)
                dve.tensor_tensor(ssq[:, :], ssq[:, :], ssq_part[:, :], ALU.add).then_inc(v_sum, 1)

            def split_product(s, it, j, lo, hi_part, in1, up):
                h, f = divmod(j, 2)
                ge(dve, s.lo, it * 4 + (j - 1))
                dve.tensor_tensor(full[f][:, :], up, in1, ALU.mult).then_inc(s.full, 1)
                dve.wait_ge(s.hi, it * 4 + (j + 1))
                dve.tensor_tensor(lo[:, f, toks(h)], full[f][:, :], r32(hi_part[:, f, toks(h)]),
                                  ALU.subtract).then_inc(s.lo, 1)

            def adds(s, it):
                def add(h, n):
                    d = 8 * h + n
                    dve.wait_ge(s.down, it * 16 + (d + 1))
                    dve.tensor_tensor(x[:, n, toks(h)], bank[4 + d % 4][:, :], x[:, n, toks(h)],
                                      ALU.add).then_inc(s.added, 1)
                return add

            def all_adds(s, it):
                add = adds(s, it)
                for h in range(NH2):
                    for k in range(KT):
                        add(h, k)

            def gmlp(it, first, last):
                s = hid["G"]
                dve.wait_ge(ws_in, (it + 1) * 32)
                dve.memset(ws_raw[CHUNK:P, 0:CHUNK], 0.0).then_inc(ws_masked, 1)
                dve.wait_ge(ws_hi_done, it + 1)
                dve.tensor_tensor(ws_lo[:, :], ws_raw[:, :], r32(ws_hi[:, :]), ALU.subtract).then_inc(ws_lo_done, 1)

                def event(j):
                    h, f = divmod(j, 2)
                    if f == 0:
                        for t in range(4):
                            dve.wait_ge(vs_hi, it * 8 + (4 * h + t + 1))
                            dve.scalar_tensor_tensor(v_lo[:, t, :], v_raw[h][:, t, :], rv[:, 4 * h + t:4 * h + t + 1],
                                                     r32(v_hi[:, t, :]), ALU.mult, ALU.subtract).then_inc(vs_lo, 1)
                    dve.wait_ge(s.mm, it * 4 + (j + 1))
                    ge(dve, s.full, it * 4 + j)
                    g_col = vgain[:, 2 * it + f:2 * it + f + 1] if isinstance(it, int) else vgain[:, bass.ds(it * 2 + f, 1)]
                    dve.scalar_tensor_tensor(tiled(mixed[:, :]), tiled(bank[2 * f][:, :]), g_col,
                                             bs[:, None, :].broadcast_to([P, 4, P]), ALU.mult, ALU.add).then_inc(mix_done, 1)
                    dve.wait_ge(mix_done, it * 4 + (j + 1))
                    dve.wait_ge(s.act, it * 4 + (j + 1))
                    split_product(s, it, j, y_lo, y_hi, atmp[f][:, :], mixed[:, :])

                for j in range(3):
                    event(j)
                if last:
                    last_half(s, it, 1, adds(s, it), lambda: event(3))
                else:
                    event(3)
                    all_adds(s, it)

            def ffn(name, n):
                def one(it, first, last):
                    s = hid[name]

                    def event(j):
                        f = j % 2
                        dve.wait_ge(s.act, it * 4 + (j + 1))
                        split_product(s, it, j, h_lo, h_hi, atmp[f][:, :], bank[2 * f + 1][:, :])

                    for j in range(3):
                        event(j)
                        if first and j == 0:
                            dve.wait_ge(s.lo, 1)
                            tiles(n - 1, 1)
                            dve.wait_ge(hn_done, 16 * n)
                    if last:
                        last_half(s, it, n, adds(s, it), lambda: event(3))
                        if n == 4:
                            for k in range(Y_DVE):
                                dve.scalar_tensor_tensor(x[:, k, toks(1)], x[:, k, toks(1)], gain[:, 4, k:k + 1],
                                                         rstd[1][:, :], ALU.mult, ALU.mult).then_inc(y_full, 1)
                    else:
                        event(3)
                        all_adds(s, it)
                return one

            def p_lo_part(it, what, i, number, dst, hi_part, src=None):
                src = src if src is not None else p_bank(it, what, i)[:, :]
                dve.wait_ge(p_hi, it * 6 + (2 + number))
                dve.tensor_tensor(dst, src, hi_part, ALU.subtract).then_inc(p_read, 1)

            def query_lo(it, h, name="q", number=None):
                dve.wait_ge(p_hi, it * 6 + (2 + 5 + h) if number is None else number)
                dve.scalar_tensor_tensor(flipped(q_lo[:, toks(h)]), tiled(p_bank(it, name, h)[:, :]), HD ** -0.5,
                                         flipped(r32(q_hi[:, toks(h)])), ALU.mult, ALU.subtract).then_inc(p_read, 1)

            def mask_bias(it):
                dve.wait_ge(bias_in, (it + 1) * 16)
                dve.memset(bias[CHUNK:P, :, WIN - CHUNK:WIN], MASKED).then_inc(bias_masked, 1)
                dve.memset(bias[0:CHUNK, :, 0:CHUNK], MASKED).then_inc(bias_masked, 1)

            def attention(it, first, last):
                def out_add(name, h, n):
                    dve.wait_ge(p_done, p_number(it, name, n) + 1)
                    dve.tensor_tensor(x[:, n, toks(h)], p_bank(it, name, n)[:, :], x[:, n, toks(h)],
                                      ALU.add).then_inc(p_read, 1)

                def v_copy(h):
                    dve.wait_ge(p_done, p_number(it, "v", h) + 1)
                    dve.tensor_copy(atmp[h][:, :], p_bank(it, "v", h)[:, :]).then_inc(p_read, 1)

                def keys_lo(h, number):
                    p_lo_part(it, "k", h, number, k_lo[:, toks(h)], r32(k_hi[:, toks(h)]))

                if first:
                    query_lo(-1, 0, "q", 1)
                    keys_lo(0, 0)
                    v_copy(0)
                    tiles(2, 1)
                    query_lo(0, 1, "q first", 3)
                    keys_lo(1, 2)
                    for part in (vz_hi, vz_lo):
                        for head in range(2):
                            dve.memset(r32(part[:, :, head, (1 - head) * HD:(2 - head) * HD]), 0.0).then_inc(vz_zero, 1)
                    mask_bias(0)
                else:
                    for h in range(NH2):
                        keys_lo(h, 1 + h)
                    v_copy(0)
                for m in range(19):
                    if 0 <= m - 1 < 16:
                        s = m - 1
                        c = slice(s % 2, s % 2 + 1)
                        dve.wait_ge(exp_done, it * 16 + (s + 1))
                        dve.reciprocal(rowinv[:, c], rowsum[:, c]).then_inc(inv_done, 1)
                    if 0 <= m - 2 < 16:
                        s = m - 2
                        dve.wait_ge(pt_hi_done, it * 16 + (s + 1))
                        dve.tensor_tensor(pt_tiles(pt_lo, s), tiled(probs_t[:, window(s):WIN]),
                                          r32(pt_tiles(pt_hi, s)), ALU.subtract).then_inc(pt_lo_done, 1)
                    if m < 16:
                        off = window(m)
                        c = slice(m % 2, m % 2 + 1)
                        dve.wait_ge(qk_done, it * 16 + (m + 1))
                        if m == 0:
                            dve.wait_ge(bias_masked, it * 2 + 2)
                        ge(dve, t_done, it * 16 + (m - 1))
                        dve.sem_inc(step_begun)
                        dve.tensor_tensor_reduce(prob[m % 2][:, off:], scores[:, SHIFT + off:SHIFT + WIN],
                                                 bias[:, step(m)[1], off:], 1.0, -3.0e38, ALU.add, ALU.max,
                                                 rowmax[:, c]).then_inc(biased, 1)
                        dve.wait_ge(biased, it * 16 + (m + 1))
                        dve.tensor_scalar(negmax[:, c], rowmax[:, c], -1.0, None, ALU.mult).then_inc(neg_done, 1)
                    if m >= 14 and last:
                        add_squares(3, 0, m - 13)
                    if m in (2, 3):
                        h = m - 2
                        p_lo_part(it, "vt", h, 3 + h, in_heads(vz_lo, h), in_heads(vz_hi, h, r32),
                                  by_head(p_bank(it, "vt", h)))
                    if m == 2:
                        v_copy(1)
                    if m == 14 and not last:
                        query_lo(it, 0)
                    for n in OUT1P.get(m, ()) if not first else ():
                        out_add("out1p", 1, n)
                    if m in (10, 18):
                        dve.wait_ge(o_hi_done, it * 2 + (1 if m == 10 else 2))
                        dve.tensor_tensor(flipped(o_lo[:, :]), tiled(bank[3][:, :]), flipped(r32(o_hi[:, :])),
                                          ALU.subtract).then_inc(o_lo_done, 1)
                    for n in OUT0.get(m, ()):
                        out_add("out0", 0, n)
                if not last:
                    mask_bias(it + 1)
                    query_lo(it, 1)
                    return
                for k in (6, 7):
                    add_squares(3, 0, k)
                for k in range(2):
                    out_add("out1", 1, k)
                inverse(3, 0)
                ops = tile_ops(3, 0)
                for k in range(2, KT):
                    ops.pop(0)()
                    out_add("out1", 1, k)
                for op in ops:
                    op()
                sum_squares(3, 1)
                inverse(3, 1)

            dve.memset(ones[:, :], 1.0 / D)
            dve.memset(eps[:, :], EPS)
            dve.memset(ssq[:, :], 0.0)
            dve.drain().then_inc(consts, 1)
            sum_squares(0, 0)
            dve.wait_ge(rel_in, 16)
            lead = WIN - P - 1
            dve.tensor_copy(rel_pad[:, 0:lead], rel[:, 0:1].broadcast_to([HEADS, lead])).then_inc(rel_padded, 1)
            dve.tensor_copy(rel_pad[:, lead:lead + N_REL], rel).then_inc(rel_padded, 1)
            dve.tensor_copy(rel_pad[:, lead + N_REL:], rel[:, N_REL - 1:N_REL].broadcast_to([HEADS, REV - lead - N_REL])
                            ).then_inc(rel_padded, 1)
            dve.wait_ge(small_in, 48)
            for h in range(NH2):
                if h == 1:
                    sum_squares(0, 1)
                inverse(0, h)
                tiles(0, h)
            repeat(dve, CB, v_block)
            dve.wait_ge(rv_std, 1)
            dve.reciprocal(rv[:, :], rv[:, :]).then_inc(rv_done, 1)
            dve.wait_ge(rv_done, 1)
            repeat(dve, GROUPS, gmlp)
            repeat(dve, CHUNKS, ffn("F1", 2))
            repeat(dve, PAIRS, attention)
            repeat(dve, CHUNKS, ffn("F2", 4))


def kernel(x, norm_mix_g, norm_ffn_g, final_g, a_w_in, a_v_gain, a_w_s, a_b_s, a_w_out, b_w_qkv, b_rel_bias,
           b_w_out, ffn_w_gate, ffn_w_up, ffn_w_down):
    import numpy as np
    import concourse.bacc as bacc
    from concourse.bass_utils import run_bass_kernel_spmd

    def tile_of(w, n):
        return w[:, n * P:(n + 1) * P].reshape(KT, P, P).transpose(1, 0, 2).reshape(P, UNIT)

    def rows_of(w, n):
        return w[n * P:(n + 1) * P, :]

    a = [np.asarray(t) for t in (a_w_in, a_w_out, b_w_qkv, b_w_out, ffn_w_gate, ffn_w_up, ffn_w_down)]
    w_in, w_out, w_qkv, w_o = (t[0] for t in a[:4])
    gate, up, down = a[4:]
    units = np.empty((UNITS, P, UNIT), np.float32)
    at = 0

    def put(unit):
        nonlocal at
        units[at] = unit
        at += 1

    for cb in range(CB):
        for j in range(4):
            v = w_in[2 * j * P:(2 * j + 2) * P, GMLP + cb * 512:GMLP + (cb + 1) * 512]
            put(v.reshape(2, P, 512).transpose(1, 0, 2).reshape(P, UNIT))
    for g in range(GROUPS):
        put(tile_of(w_in, 2 * g)), put(tile_of(w_in, 2 * g + 1))
        put(rows_of(w_out, 2 * g)), put(rows_of(w_out, 2 * g + 1))

    def ffn(i):
        for c in range(CHUNKS):
            for f in (2 * c, 2 * c + 1):
                put(tile_of(gate[i], f)), put(tile_of(up[i], f))
            put(rows_of(down[i], 2 * c)), put(rows_of(down[i], 2 * c + 1))

    ffn(0)
    put(tile_of(w_qkv, 0))
    for pair in range(PAIRS):
        put(tile_of(w_qkv, KT + pair)), put(tile_of(w_qkv, 2 * KT + pair))
        if pair < PAIRS - 1:
            put(tile_of(w_qkv, pair + 1))
        put(rows_of(w_o, pair))
    ffn(1)

    g = np.stack([np.asarray(t) for t in (norm_mix_g[0], norm_ffn_g[0], norm_mix_g[1], norm_ffn_g[1], final_g)])
    arrays = {
        "x_t": np.asarray(x)[0].T.reshape(KT, P, SEQ),
        "gains": g.reshape(5, KT, P).transpose(2, 0, 1),
        "v_gain": np.asarray(a_v_gain)[0].reshape(GMLP // P, P).T,
        "w_s_t": np.asarray(a_w_s)[0].transpose(0, 2, 1),
        "b_s": np.asarray(a_b_s)[0],
        "rel_rev": np.asarray(b_rel_bias)[0][:, ::-1],
        "ident": np.eye(P, dtype=np.float32),
        "w_units": units,
    }
    arrays = {name: np.ascontiguousarray(t) for name, t in arrays.items()}
    nc = bacc.Bacc("TRN2", target_bir_lowering=False, num_devices=1)
    ins = [nc.dram_tensor(name + "_in", t.shape, F32, kind="ExternalInput").ap() for name, t in arrays.items()]
    out = nc.dram_tensor("out_t", (KT, P, SEQ), F32, kind="ExternalOutput").ap()
    trunk(nc, *ins, out)
    r = run_bass_kernel_spmd(nc, [{name + "_in": t for name, t in arrays.items()}], core_ids=[0])
    return np.ascontiguousarray(r.results[0]["out_t"].reshape(D, SEQ).T).reshape(1, SEQ, D)
```
